# Optimizing a Trainium2 kernel written in Bass

```python
import math
import jax, jax.numpy as jnp
from jax import lax
import numpy as np

D_MODEL = 1024
BATCH = 1
SEQ = 256
DEPTH = 1

CHUNK = 64
N_META = 16
N_HEADS = 8
HEAD_DIM = 64
V_HEAD_DIM = 2 * HEAD_DIM
ATT_QK = N_HEADS * 2 * HEAD_DIM
ATT_V = N_HEADS * V_HEAD_DIM
CONV_CH = D_MODEL
CONV_K = 31
D_FF = 2816
FFN_CONV_K = 3
QB = 128
NEG_INF = -1e30
IN_COLS = 2 * ATT_QK + ATT_V + 2 * CONV_CH + 2 * D_MODEL


def _rms(x, w, eps=1e-6):
    xf = x.astype(jnp.float32)
    y = xf * lax.rsqrt(jnp.mean(xf * xf, axis=-1, keepdims=True) + eps)
    return (y * w.astype(jnp.float32)).astype(x.dtype)

def _layernorm(x, w, b, eps=1e-5):
    xf = x.astype(jnp.float32)
    mu = jnp.mean(xf, axis=-1, keepdims=True)
    xc = xf - mu
    y = xc * lax.rsqrt(jnp.mean(xc * xc, axis=-1, keepdims=True) + eps)
    return (y * w.astype(jnp.float32) + b.astype(jnp.float32)).astype(x.dtype)

def _causal_dwconv(x, w, b):
    k, c = w.shape
    y = lax.conv_general_dilated(
        x, w[:, None, :].astype(x.dtype), window_strides=(1,), padding=[(k - 1, 0)],
        dimension_numbers=('NWC', 'WIO', 'NWC'), feature_group_count=c)
    return y + b.astype(x.dtype)

def _diff_attention(q, k, v, lam, cid):
    b, lp = q.shape[0], q.shape[1]
    nblk = lp // QB
    qf = q.astype(jnp.float32) * (HEAD_DIM ** -0.5)
    kf = k.astype(jnp.float32)
    vf = v.astype(jnp.float32)

    def block(i):
        start = i * QB
        qb = lax.dynamic_slice_in_dim(qf, start, QB, axis=1)
        qc = lax.dynamic_slice_in_dim(cid, start, QB, axis=0)
        s = jnp.einsum('bqhmd,bkhmd->bhmqk', qb, kf)
        mask = cid[None, :] <= qc[:, None]
        p = jax.nn.softmax(jnp.where(mask, s, NEG_INF), axis=-1)
        a = p[:, :, 0] - lam * p[:, :, 1]
        return jnp.einsum('bhqk,bkhe->bqhe', a, vf)

    o = lax.map(block, jnp.arange(nblk))
    return jnp.moveaxis(o, 0, 1).reshape(b, lp, N_HEADS, V_HEAD_DIM)

def first_inputs(seed: int = 0) -> dict:
    key = jax.random.key(seed)
    ks = jax.random.split(key, 24)
    f32 = jnp.float32
    nrm = lambda k, shape, scale: (jax.random.normal(k, shape, f32) * scale)
    gain = lambda k, shape: 1.0 + 0.05 * jax.random.normal(k, shape, f32)
    L = DEPTH
    return {
        "x": nrm(ks[0], (BATCH, SEQ, D_MODEL), 1.0),
        "meta_tokens": nrm(ks[1], (N_META, D_MODEL), 0.5),
        "norm_mix_w": gain(ks[2], (L, D_MODEL)),
        "w_in": nrm(ks[3], (L, D_MODEL, IN_COLS), D_MODEL ** -0.5),
        "lambda_q1": nrm(ks[4], (L, HEAD_DIM), 0.1),
        "lambda_k1": nrm(ks[5], (L, HEAD_DIM), 0.1),
        "lambda_q2": nrm(ks[6], (L, HEAD_DIM), 0.1),
        "lambda_k2": nrm(ks[7], (L, HEAD_DIM), 0.1),
        "subln_w": gain(ks[8], (L, V_HEAD_DIM)),
        "conv_dw_w": nrm(ks[9], (L, CONV_K, CONV_CH), CONV_K ** -0.5),
        "conv_dw_b": nrm(ks[10], (L, CONV_CH), 0.02),
        "conv_ln_w": gain(ks[11], (L, CONV_CH)),
        "conv_ln_b": nrm(ks[12], (L, CONV_CH), 0.02),
        "w_conv_out": nrm(ks[13], (L, CONV_CH, D_MODEL), CONV_CH ** -0.5),
        "w_out": nrm(ks[14], (L, D_MODEL, D_MODEL), D_MODEL ** -0.5),
        "norm_ffn_w": gain(ks[15], (L, D_MODEL)),
        "w_up": nrm(ks[16], (L, D_MODEL, 2 * D_FF), D_MODEL ** -0.5),
        "ffn_dw_w": nrm(ks[17], (L, FFN_CONV_K, 2 * D_FF), FFN_CONV_K ** -0.5),
        "ffn_dw_b": nrm(ks[18], (L, 2 * D_FF), 0.02),
        "w_down": nrm(ks[19], (L, D_FF, D_MODEL), D_FF ** -0.5),
        "norm_final_w": gain(ks[20], (D_MODEL,)),
    }

def first_block(x, meta_tokens, norm_mix_w, w_in, lambda_q1, lambda_k1, lambda_q2, lambda_k2,
              subln_w, conv_dw_w, conv_dw_b, conv_ln_w, conv_ln_b, w_conv_out, w_out,
              norm_ffn_w, w_up, ffn_dw_w, ffn_dw_b, w_down, norm_final_w):
    b, s, d = x.shape
    total = s + N_META
    lp = ((total + QB - 1) // QB) * QB
    meta = jnp.broadcast_to(meta_tokens[None].astype(x.dtype), (b, N_META, d))
    h = jnp.concatenate([meta, x], axis=1)
    h = jnp.pad(h, ((0, 0), (0, lp - total), (0, 0)))
    pos = jnp.arange(lp)
    cid = jnp.where(pos < N_META, 0, (pos - N_META) // CHUNK + 1)

    splits = [ATT_QK, 2 * ATT_QK, 2 * ATT_QK + ATT_V,
              2 * ATT_QK + ATT_V + 2 * CONV_CH, 2 * ATT_QK + ATT_V + 2 * CONV_CH + D_MODEL]
    for l in range(DEPTH):
        lambda_init = 0.8 - 0.6 * math.exp(-0.3 * l)
        n = _rms(h, norm_mix_w[l])
        z = n @ w_in[l]
        q, k, v, glu, g_att, g_conv = jnp.split(z, splits, axis=-1)
        lam = (jnp.exp(jnp.sum(lambda_q1[l].astype(jnp.float32) * lambda_k1[l].astype(jnp.float32)))
               - jnp.exp(jnp.sum(lambda_q2[l].astype(jnp.float32) * lambda_k2[l].astype(jnp.float32)))
               + lambda_init)
        q = q.reshape(b, lp, N_HEADS, 2, HEAD_DIM)
        k = k.reshape(b, lp, N_HEADS, 2, HEAD_DIM)
        v = v.reshape(b, lp, N_HEADS, V_HEAD_DIM)
        o = _diff_attention(q, k, v, lam, cid)
        y_att = (_rms(o, subln_w[l]) * (1.0 - lambda_init)).reshape(b, lp, ATT_V).astype(h.dtype)
        u = glu[..., :CONV_CH] * jax.nn.sigmoid(glu[..., CONV_CH:])
        u = _causal_dwconv(u, conv_dw_w[l], conv_dw_b[l])
        u = jax.nn.silu(_layernorm(u, conv_ln_w[l], conv_ln_b[l]))
        y_conv = u @ w_conv_out[l]
        m = jax.nn.sigmoid(g_att) * y_att + jax.nn.sigmoid(g_conv) * y_conv
        h = h + m @ w_out[l]
        n2 = _rms(h, norm_ffn_w[l])
        up = _causal_dwconv(n2 @ w_up[l], ffn_dw_w[l], ffn_dw_b[l])
        gate, val = jnp.split(up, 2, axis=-1)
        h = h + (jax.nn.silu(gate) * val) @ w_down[l]

    out = _rms(h, norm_final_w)
    return out[:, N_META:N_META + s]


N_MEM = 256
EPS = 1e-6
NEG = -1e30

A_HEADS = 16
A_HEAD_DIM = 64
A_WIDTH = A_HEADS * A_HEAD_DIM
MOBA_BLOCK = 256
MOBA_TOPK = 3
MOBA_Q_CHUNK = 32
ROPE_THETA = 10000.0

B_HEADS = 8
B_KEY_DIM = 128
B_VAL_DIM = D_MODEL // B_HEADS
B_KEY_WIDTH = B_HEADS * B_KEY_DIM
B_VAL_WIDTH = B_HEADS * B_VAL_DIM
HGRN_CHUNK = 64

X_HEADS = 4
X_HEAD_DIM = D_MODEL // X_HEADS

FFN_HIDDEN = ((8 * D_MODEL + 3 * 256 - 1) // (3 * 256)) * 256

IN_WIDTHS = (A_WIDTH, A_WIDTH, A_WIDTH, B_KEY_WIDTH, B_KEY_WIDTH, B_VAL_WIDTH, B_VAL_WIDTH, D_MODEL, D_MODEL)
IN_WIDTH = A_WIDTH * 3 + B_KEY_WIDTH * 2 + B_VAL_WIDTH * 2 + D_MODEL * 2


def rmsnorm(x, g):
    xf = x.astype(jnp.float32)
    y = xf * lax.rsqrt(jnp.mean(xf * xf, axis=-1, keepdims=True) + EPS)
    return (y * g.astype(jnp.float32)).astype(x.dtype)

def rope(t, pos):
    hd = t.shape[-1]
    inv_freq = jnp.power(ROPE_THETA, -jnp.arange(0, hd, 2, dtype=jnp.float32) / hd)
    ang = pos.astype(jnp.float32)[:, None, :, None] * inv_freq
    cos, sin = jnp.cos(ang), jnp.sin(ang)
    tf = t.astype(jnp.float32)
    t1, t2 = tf[..., : hd // 2], tf[..., hd // 2:]
    return jnp.concatenate([t1 * cos - t2 * sin, t2 * cos + t1 * sin], axis=-1).astype(t.dtype)

def split_cols(z):
    outs, off = [], 0
    for w in IN_WIDTHS:
        outs.append(z[..., off:off + w])
        off += w
    return outs

def moba_attention(q, k, v, pos):
    B, S, _ = q.shape
    H, hd, BLK, QC = A_HEADS, A_HEAD_DIM, MOBA_BLOCK, MOBA_Q_CHUNK
    scale = hd ** -0.5

    def heads(t):
        return t.reshape(B, S, H, hd).transpose(0, 2, 1, 3)

    q = rope(heads(q), pos)
    k = rope(heads(k), pos)
    v = heads(v)
    nb = -(-S // BLK)
    s_pad = nb * BLK
    padw = [(0, 0), (0, 0), (0, s_pad - S), (0, 0)]
    q, k, v = jnp.pad(q, padw), jnp.pad(k, padw), jnp.pad(v, padw)
    kb = k.reshape(B, H, nb, BLK, hd)
    vb = v.reshape(B, H, nb, BLK, hd)

    k_mean = jnp.mean(kb.astype(jnp.float32), axis=3)
    gate = jnp.einsum('bhsd,bhnd->bhsn', q.astype(jnp.float32), k_mean)
    q_blk = jnp.arange(s_pad) // BLK
    past = jnp.arange(nb)[None, :] < q_blk[:, None]
    gate = jnp.where(past, gate, NEG)
    n_sel = min(MOBA_TOPK, nb)
    _, idx = lax.top_k(gate, n_sel)
    valid = idx < q_blk[:, None]

    n_chunks = s_pad // QC

    def to_chunks(t):
        return jnp.moveaxis(t.reshape(B, H, n_chunks, QC, t.shape[-1]), 2, 0)

    starts = jnp.arange(n_chunks, dtype=jnp.int32) * QC
    bi = jnp.arange(B)[:, None, None, None]
    hi = jnp.arange(H)[None, :, None, None]

    def attend(args):
        qc, ic, vmask, start = args
        blk = start // BLK
        k_own = lax.dynamic_index_in_dim(kb, blk, axis=2, keepdims=False)
        v_own = lax.dynamic_index_in_dim(vb, blk, axis=2, keepdims=False)
        q_pos = start + jnp.arange(QC)
        k_pos = blk * BLK + jnp.arange(BLK)
        s_own = jnp.einsum('bhqd,bhkd->bhqk', qc, k_own).astype(jnp.float32) * scale
        s_own = jnp.where(k_pos[None, :] <= q_pos[:, None], s_own, NEG)
        k_sel = kb[bi, hi, ic]
        v_sel = vb[bi, hi, ic]
        s_sel = jnp.einsum('bhqd,bhqjkd->bhqjk', qc, k_sel).astype(jnp.float32) * scale
        s_sel = jnp.where(vmask[..., None], s_sel, NEG).reshape(B, H, QC, n_sel * BLK)
        p = jax.nn.softmax(jnp.concatenate([s_sel, s_own], axis=-1), axis=-1).astype(v.dtype)
        p_sel = p[..., : n_sel * BLK].reshape(B, H, QC, n_sel, BLK)
        p_own = p[..., n_sel * BLK:]
        return (jnp.einsum('bhqjk,bhqjkd->bhqd', p_sel, v_sel)
                + jnp.einsum('bhqk,bhkd->bhqd', p_own, v_own))

    o = lax.map(attend, (to_chunks(q), to_chunks(idx), to_chunks(valid), starts))
    o = jnp.moveaxis(o, 0, 2).reshape(B, H, s_pad, hd)[:, :, :S]
    return o.transpose(0, 2, 1, 3).reshape(B, S, H * hd)

def hgrn2(q, f, i, og, lb, norm_g):
    B, S, _ = q.shape
    H, dk, dv, C = B_HEADS, B_KEY_DIM, B_VAL_DIM, HGRN_CHUNK
    nc = S // C

    def heads(t, d):
        return t.reshape(B, S, H, d).transpose(0, 2, 1, 3).astype(jnp.float32)

    qh = jax.nn.silu(heads(q, dk)) * (dk ** -0.5)
    lbh = lb.astype(jnp.float32).reshape(1, H, 1, dk)
    fg = lbh + (1.0 - lbh) * jax.nn.sigmoid(heads(f, dk))
    logf = jnp.log(fg)
    kh = 1.0 - fg
    vh = heads(i, dv)

    def to_chunks(t):
        return jnp.moveaxis(t.reshape(B, H, nc, C, t.shape[-1]), 2, 0)

    causal = jnp.tril(jnp.ones((C, C), dtype=bool))[:, :, None]

    def step(state, xs):
        qc, kc, vc, gc = xs
        b = jnp.cumsum(gc, axis=2)
        o_inter = jnp.einsum('bhtd,bhdv->bhtv', qc * jnp.exp(b), state)
        diff = b[:, :, :, None, :] - b[:, :, None, :, :]
        decay = jnp.where(causal, jnp.exp(jnp.where(causal, diff, 0.0)), 0.0)
        a = jnp.einsum('bhtd,bhsd,bhtsd->bhts', qc, kc, decay)
        o = o_inter + jnp.einsum('bhts,bhsv->bhtv', a, vc)
        b_last = b[:, :, -1:, :]
        new_state = (jnp.exp(b_last[:, :, 0, :])[..., None] * state
                     + jnp.einsum('bhsd,bhsv->bhdv', kc * jnp.exp(b_last - b), vc))
        return new_state, o

    s0 = jnp.zeros((B, H, dk, dv), jnp.float32)
    _, o = lax.scan(step, s0, (to_chunks(qh), to_chunks(kh), to_chunks(vh), to_chunks(logf)))
    o = jnp.moveaxis(o, 0, 2).reshape(B, H, S, dv).transpose(0, 2, 1, 3)
    o = o * lax.rsqrt(jnp.mean(o * o, axis=-1, keepdims=True) + EPS)
    o = o.reshape(B, S, H * dv) * norm_g.astype(jnp.float32)
    o = o * jax.nn.silu(og.astype(jnp.float32))
    return o.astype(q.dtype)

def memory_cross_attention(h, mem, wq, wkv, wo):
    B, S, _ = h.shape
    M = mem.shape[1]
    q = (h @ wq).reshape(B, S, X_HEADS, X_HEAD_DIM)
    kv = mem @ wkv
    k = kv[..., :D_MODEL].reshape(B, M, X_HEADS, X_HEAD_DIM)
    v = kv[..., D_MODEL:].reshape(B, M, X_HEADS, X_HEAD_DIM)
    s = jnp.einsum('bshd,bmhd->bhsm', q, k).astype(jnp.float32) * (X_HEAD_DIM ** -0.5)
    p = jax.nn.softmax(s, axis=-1).astype(v.dtype)
    o = jnp.einsum('bhsm,bmhd->bshd', p, v).reshape(B, S, D_MODEL)
    return o @ wo

def second_inputs(seed: int = 0) -> dict:
    key = jax.random.key(seed)
    ks = jax.random.split(key, 24)
    f32 = jnp.float32

    def w(k, shape, fan_in):
        return jax.random.normal(k, shape, f32) * (fan_in ** -0.5)

    def gain(k, shape):
        return 1.0 + 0.02 * jax.random.normal(k, shape, f32)

    x = jax.random.normal(ks[0], (BATCH, SEQ, D_MODEL), f32)
    mem = jax.random.normal(ks[1], (BATCH, N_MEM, D_MODEL), f32)
    offs = jax.random.randint(ks[2], (BATCH, 1), 0, 1024, dtype=jnp.int32)
    positions = offs + jnp.arange(SEQ, dtype=jnp.int32)[None, :]
    return {
        "x": x,
        "mem": mem,
        "positions": positions,
        "norm_mix_g": gain(ks[3], (DEPTH, D_MODEL)),
        "w_in": w(ks[4], (DEPTH, D_MODEL, IN_WIDTH), D_MODEL),
        "hgrn_lb_logits": 0.5 * jax.random.normal(ks[5], (DEPTH + 1, B_KEY_WIDTH), f32),
        "hgrn_norm_g": gain(ks[6], (DEPTH, B_VAL_WIDTH)),
        "w_br_attn": w(ks[7], (DEPTH, A_WIDTH, D_MODEL), A_WIDTH),
        "w_br_hgrn": w(ks[8], (DEPTH, B_VAL_WIDTH, D_MODEL), B_VAL_WIDTH),
        "w_out": w(ks[9], (DEPTH, D_MODEL, D_MODEL), D_MODEL),
        "norm_x_g": gain(ks[10], (DEPTH, D_MODEL)),
        "norm_mem_g": gain(ks[11], (DEPTH, D_MODEL)),
        "wq_x": w(ks[12], (DEPTH, D_MODEL, D_MODEL), D_MODEL),
        "wkv_x": w(ks[13], (DEPTH, D_MODEL, 2 * D_MODEL), D_MODEL),
        "wo_x": w(ks[14], (DEPTH, D_MODEL, D_MODEL), D_MODEL),
        "norm_ffn_g": gain(ks[15], (DEPTH, D_MODEL)),
        "w_ffn_in": w(ks[16], (DEPTH, D_MODEL, 2 * FFN_HIDDEN), D_MODEL),
        "w_ffn_out": w(ks[17], (DEPTH, FFN_HIDDEN, D_MODEL), FFN_HIDDEN),
        "final_norm_g": gain(ks[18], (D_MODEL,)),
    }

def second_block(x, mem, positions, norm_mix_g, w_in, hgrn_lb_logits, hgrn_norm_g, w_br_attn,
              w_br_hgrn, w_out, norm_x_g, norm_mem_g, wq_x, wkv_x, wo_x, norm_ffn_g,
              w_ffn_in, w_ffn_out, final_norm_g):
    lb_all = jnp.cumsum(jax.nn.softmax(hgrn_lb_logits.astype(jnp.float32), axis=0), axis=0)
    h = x
    for l in range(DEPTH):
        xn = rmsnorm(h, norm_mix_g[l])
        q_a, k_a, v_a, q_b, f_b, i_b, og_b, g_a, g_b = split_cols(xn @ w_in[l])
        y_a = moba_attention(q_a, k_a, v_a, positions) @ w_br_attn[l]
        y_b = hgrn2(q_b, f_b, i_b, og_b, lb_all[l], hgrn_norm_g[l]) @ w_br_hgrn[l]
        merged = jax.nn.sigmoid(g_a) * y_a + jax.nn.sigmoid(g_b) * y_b
        h = h + merged @ w_out[l]
        h = h + memory_cross_attention(rmsnorm(h, norm_x_g[l]), rmsnorm(mem, norm_mem_g[l]),
                                       wq_x[l], wkv_x[l], wo_x[l])
        hn = rmsnorm(h, norm_ffn_g[l])
        gu = hn @ w_ffn_in[l]
        h = h + (jax.nn.silu(gu[..., :FFN_HIDDEN]) * gu[..., FFN_HIDDEN:]) @ w_ffn_out[l]
    return rmsnorm(h, final_norm_g)


def setup_inputs(seed=0):
    out = dict(first_inputs(seed))
    for name, value in second_inputs(seed + 1).items():
        if name != "x":
            out[name + "_2"] = value
    return out


def reference(
    x, meta_tokens, norm_mix_w, w_in, lambda_q1, lambda_k1, lambda_q2, lambda_k2, subln_w,
    conv_dw_w, conv_dw_b, conv_ln_w, conv_ln_b, w_conv_out, w_out, norm_ffn_w, w_up, ffn_dw_w,
    ffn_dw_b, w_down, norm_final_w, mem_2, positions_2, norm_mix_g_2, w_in_2, hgrn_lb_logits_2,
    hgrn_norm_g_2, w_br_attn_2, w_br_hgrn_2, w_out_2, norm_x_g_2, norm_mem_g_2, wq_x_2, wkv_x_2,
    wo_x_2, norm_ffn_g_2, w_ffn_in_2, w_ffn_out_2, final_norm_g_2,
):
    x = first_block(
        x, meta_tokens, norm_mix_w, w_in, lambda_q1, lambda_k1, lambda_q2, lambda_k2, subln_w,
        conv_dw_w, conv_dw_b, conv_ln_w, conv_ln_b, w_conv_out, w_out, norm_ffn_w, w_up,
        ffn_dw_w, ffn_dw_b, w_down, norm_final_w,
    )
    return second_block(
        x, mem_2, positions_2, norm_mix_g_2, w_in_2, hgrn_lb_logits_2, hgrn_norm_g_2,
        w_br_attn_2, w_br_hgrn_2, w_out_2, norm_x_g_2, norm_mem_g_2, wq_x_2, wkv_x_2, wo_x_2,
        norm_ffn_g_2, w_ffn_in_2, w_ffn_out_2, final_norm_g_2,
    )


_drawn_inputs = setup_inputs


def setup_inputs(seed=0):
    import zlib

    import numpy as np

    out = dict(_drawn_inputs(seed))
    spreads = {}
    factors = {'lambda_k1': 3.355,
     'lambda_q2': 3.542,
     'conv_dw_b': 3.691,
     'conv_ln_b': 6.857,
     'ffn_dw_b': 3.499,
     'norm_mix_g_2': 5.071,
     'hgrn_lb_logits_2': 3.103,
     'hgrn_norm_g_2': 8.0,
     'norm_x_g_2': 8.0,
     'norm_mem_g_2': 8.0,
     'norm_ffn_g_2': 16.42,
     'final_norm_g_2': 7.768}
    for name, (base, spread) in spreads.items():
        noise = np.random.default_rng([zlib.crc32(name.encode()), seed]).standard_normal(out[name].shape)
        drawn = base * np.exp(spread * noise) if base else spread * noise
        out[name] = __import__('jax').numpy.asarray(drawn.astype(out[name].dtype))
    for name, factor in factors.items():
        out[name] = (out[name] * factor).astype(out[name].dtype)
    return out
```

```python
from contextlib import ExitStack

import concourse.bass as bass
from concourse import mybir

F32 = mybir.dt.float32
I32 = mybir.dt.int32
ALU = mybir.AluOpType
ACT = mybir.ActivationFunctionType
AX = mybir.AxisListType.X

P = 128
D = 1024
KB = D // P
SEQ = 256
META = 16
T1 = META + SEQ
LEAD = 2
Q0 = META - LEAD
TQ = T1 - Q0
HEADS = 8
HD = 64
CHUNK = 64
TAPS = 31
FF = 2816
FT = FF // P
NEG = -1e30
LAMBDA_INIT = 0.8 - 0.6
MAGIC = 1.5 * 2.0 ** 23
TWO_PI = (6.28125, 0.0019350051879882812, 3.0199159819e-07)
PI_IN = 3.1415925
LEVELS = (64, 32, 16, 8, 4, 2, 1)
RING = 8
KEY_SCALE = 0.5 * P ** -0.5
LOG_MIN = 2.0 ** -63
NORMS = {"mix1": 0, "mem": 1, "ffn1": 2, "final1": 3, "mix2": 4, "cross": 5, "ffn2": 6, "out": 7}
CW = 2 * P

TABLE = [
    ("norm_mix_w", KB), ("subln_w", 1), ("conv_dw_w", KB * TAPS), ("conv_dw_b", KB), ("conv_ln_w", KB),
    ("conv_ln_b", KB), ("norm_ffn_w", KB), ("ffn_dw_w", 2 * FT * 3), ("ffn_dw_b", 2 * FT), ("norm_final_w", KB),
    ("norm_mix_g_2", KB), ("lb_logits", 2 * KB), ("hgrn_norm_g_2", KB), ("norm_x_g_2", KB), ("norm_mem_g_2", KB),
    ("norm_ffn_g_2", KB), ("final_norm_g_2", KB), ("lambdas", 4 * HD), ("ones", P), ("ident", P), ("rotate", P),
    ("inv_freq", 1), ("eps6", 1), ("eps5", 1), ("causal", P), ("level_masks", len(LEVELS) * P),
]
WIDTH = dict(TABLE)
AT = {}
TABLE_W = 0
for _name, _w in TABLE:
    AT[_name] = TABLE_W
    TABLE_W += _w

PHASES = [
    ("heads1", 4, (0, 1, 2, 3, 4), (2,) * 5),
    ("gates1", 2, (5, 6, 7, 0), (2,) * 4),
    ("mem_k", 1, (1, 2, 3, 4), (2,) * 4),
    ("mem_v", 1, (5, 6, 7, 0), (2,) * 4),
    ("conv_out", 1, (1, 2, 3, 4), (2,) * 4),
    ("mix_out1", 1, (5, 6, 7, 0), (2,) * 4),
    ("up1", 5, (1, 2, 3, 4), (2,) * 4),
    ("up1_end", 1, (5, 6), (2,) * 2),
    ("down1", 2, (7, 0, 1, 2), (1,) * 4),
    ("down1_end", 1, (3, 4, 5), (1, 1, 4)),
    ("forget", 1, (6, 7, 0, 1), (2,) * 4),
    ("heads2", 4, (2, 3, 4, 5, 6, 7, 0, 1), (2,) * 8),
    ("branch_a", 1, (2, 3, 4, 5), (2,) * 4),
    ("branch_b", 1, (6, 7, 0, 1), (2,) * 4),
    ("mix_out2", 1, (2, 3, 4, 5), (2,) * 4),
    ("cross_q", 1, (6, 7, 0, 1), (2,) * 4),
    ("cross_out", 1, (2, 3, 4, 5), (2,) * 4),
    ("up2", 5, (6, 7, 0, 1), (2,) * 4),
    ("up2_end", 1, (2, 3), (2,) * 2),
    ("down2", 2, (4, 5, 6, 7), (1,) * 4),
    ("down2_end", 1, (0, 1, 2), (1, 1, 4)),
]
TWO_BANKS = ("heads2",)


class Stream:

    def __init__(self):
        self.at = {}
        chunk, done, landed, used = 0, 0, [0] * RING, [0] * 4
        for name, iters, slots, tiles in PHASES:
            banks = []
            if not name.startswith("down"):
                banks = [t % (2 if name in TWO_BANKS else 4) for t in range(sum(tiles))]
            elif name.endswith("end"):
                banks = [0, 1, 2, 3]
            self.at[name] = (chunk, done, tuple(landed), tuple(used), iters, slots, tiles, banks)
            chunk += iters * len(slots)
            done += iters * sum(tiles)
            for s in slots:
                landed[s] += iters
            for b in banks:
                used[b] += iters
        self.chunks = chunk

    def landed(self, phase, i, c):
        _, _, landed, _, _, slots, _, _ = self.at[phase]
        return (i + (landed[slots[c]] + 1)) * 16

    def done(self, phase, i, t):
        _, done, _, _, _, _, tiles, _ = self.at[phase]
        return i * sum(tiles) + (done + t + 1)

    def bank(self, phase, t):
        return self.at[phase][7][t]

    def before(self, phase, i, t):
        _, _, _, used, _, _, _, banks = self.at[phase]
        b = banks[t]
        return i * banks.count(b) + (1 + used[b] + banks[:t].count(b))


STREAM = Stream()

CREDITED = ("tile_read", "bank_full", "bank_read", "probs_ready", "level_ready", "decay_ready", "conv_ready", "act_ready")


def credit(name):
    return 1 if name.startswith(CREDITED) else 0


BODY = {}
BODY[('tensor', 'heads1')] = {'kv_ready': 1, 'bank_read4': 4, 'probs_ready': 4, 'bank_read6': 4, 'bank_read7': 4}
BODY[('tensor', 'gates1')] = {}
BODY[('tensor', 'up1')] = {}
BODY[('tensor', 'heads2')] = {'bank_read7': 4, 'khs_ready': 2, 'level_ready': 16, 'bank_read2': 2, 'bank_read3': 4, 'bank_read4': 4, 'probs_ready': 4, 'bank_read5': 4, 'bank_read6': 2}
BODY[('tensor', 'up2')] = {}
BODY[('scalar', 'heads1')] = {'bank_full4': 4, 'max_ready': 4, 'probs_ready': 4, 'bank_full6': 4, 'bank_full7': 4}
BODY[('scalar', 'gates1')] = {}
BODY[('scalar', 'up1')] = {'act_ready0': 2, 'tap0': 8, 'gate_act': 4, 'act_ready1': 2}
BODY[('scalar', 'heads2')] = {'bank_full7': 4, 'diff_ready': 14, 'level_ready': 16, 'bank_full4': 4, 'max_ready': 8, 'bank_full3': 4, 'bank_full5': 4, 'bank_full6': 4}
BODY[('scalar', 'up2')] = {}
BODY[('vector', 'heads1')] = {'bank_full4': 4, 'dve_step': 47, 'bank_read4': 4, 'bank_full6': 4, 'conv_ready': 1}
BODY[('vector', 'conv odd a')] = {'conv_ready': 1, 'dve_step': 31}
BODY[('vector', 'conv odd b')] = {'conv_ready': 1, 'dve_step': 31}
BODY[('vector', 'up1')] = {'tap0': 8, 'dve_step': 8, 'gate_act': 4}
BODY[('vector', 'cumulate')] = {}
BODY[('vector', 'heads2')] = {'tanh_ready': 4, 'decay_ready': 16, 'bank_full2': 2, 'dve_step': 24, 'bank_full7': 4, 'bank_read7': 4, 'bank_full3': 4, 'bank_read3': 2, 'bank_full4': 4, 'bank_read4': 4}
BODY[('vector', 'up2')] = {}
BODY[('gpsimd', 'heads2')] = {'decay_ready': 16}



class Tally:

    def __init__(self, engine):
        self.engine, self.base, self.inside, self.i, self.body = engine, {}, {}, None, {}

    def before(self, sem, k=1):
        v = self.now(sem)
        (self.base if self.i is None else self.inside)[sem.name] = \
            (self.base if self.i is None else self.inside).get(sem.name, 0 if self.i is not None else credit(sem.name)) + k
        return v

    def next(self, sem, k=1):
        self.before(sem, k)
        return self.now(sem)

    def now(self, sem):
        v = self.base.get(sem.name, credit(sem.name))
        if self.i is not None:
            v = self.i * self.body.get(sem.name, 0) + (v + self.inside.get(sem.name, 0))
        return v

    def enter(self, loop, i):
        self.i, self.loop, self.inside = i, loop, {}
        self.body = BODY.get((self.engine, loop), {})

    def leave(self, iters):
        check_body(self.engine, self.loop, self.inside, self.body)
        for name, k in self.inside.items():
            self.base[name] = self.base.get(name, credit(name)) + iters * k
        self.i = None


def check_body(engine, loop, found, stated):
    assert found == stated, (engine, loop, found)


def hold(eng, sem, value):
    if not (isinstance(value, int) and value <= 0):
        eng.wait_ge(sem, value)


def blocks_kernel(nc, a):
    ctx = ExitStack()
    with ctx:
        def sb(name, shape, dt=F32):
            return ctx.enter_context(nc.sbuf_tensor(name, shape, dt))

        def sem(name):
            return ctx.enter_context(nc.semaphore(name))

        ring = sb("ring", [P, RING, KB * CW])
        table = sb("table_sb", [P, TABLE_W])
        res = sb("res", [P, KB, T1])
        res2 = sb("res2", [P, KB, SEQ])
        xT = sb("xT", [P, KB, T1])
        sq = sb("sq", [P, KB, T1])
        k_mem = sb("k_mem", [P, KB, SEQ])
        v_mem = sb("v_mem", [P, 2, D])
        glu = sb("glu", [P, KB, TAPS - 1 + T1])
        conv = sb("conv", [P, KB, TQ])
        att = sb("att", [P, HEADS, TQ])
        gates = sb("gates", [P, 2 * KB, TQ])
        act = sb("act", [P, FT, SEQ])
        work = sb("work", [P, 4864])
        root = sb("root", [P, T1])
        rinv = sb("rinv", [P, T1])
        small = sb("small", [P, 96])
        pos_i = res2[:, 0, :].bitcast(I32)
        ps = ctx.enter_context(nc.psum_tensor("ps", [P, 8, 512], F32))

        def carve(region, at, *shape):
            n = 1
            for d in shape:
                n *= d
            flat = region[:, at:at + n]
            if len(shape) == 1:
                return flat
            if len(shape) == 2:
                return flat.rearrange("p (a b) -> p a b", b=shape[1])
            return flat.rearrange("p (a b c) -> p a b c", b=shape[1], c=shape[2])

        def col(name, j=0, n=1):
            return table[:, AT[name] + j:AT[name] + j + n] if isinstance(j, int) else \
                table[:, bass.ds(j + AT[name], n)]

        ones, ident = col("ones", 0, P), col("ident", 0, P)

        qT = carve(work, 0, 2, TQ)
        kT = carve(work, 516, 2, T1)
        vN = carve(work, 1060, 2, CW)
        v_meta = carve(work, 1572, CW)
        tanh_b = carve(work, 2596, 2, T1)
        E1 = carve(work, 3140, 2, T1)
        a1 = carve(work, 3684, T1)
        a1T = carve(work, 3956, 2 * P)
        a1M = carve(work, 4212, P)
        conv_odd = carve(work, 4340, TQ)
        qM = carve(work, 4598, HEADS, LEAD)
        kM = carve(work, 4614, HEADS, META)
        sM = carve(work, 0, 2 * HEADS, META)
        aM = carve(work, 256, HEADS, META)
        aMT = carve(work, 384, HEADS, LEAD)
        taps = carve(work, 0, 8, SEQ)
        silu_g = carve(work, 2048, 4, SEQ)
        actf = act[:, :, :].rearrange("p a b -> p (a b)")
        mem = carve(actf, 0, KB, SEQ)
        att_root = carve(actf, 2048, 2, 4 * TQ)
        vM = carve(actf, 4112, D)
        bT = conv_f = conv[:, :, :].rearrange("p a b -> p (a b)")
        bT = carve(conv_f, 0, HEADS, SEQ)
        gluf = glu[:, :, :].rearrange("p a b -> p (a b)")
        kh = carve(gluf, 0, HEADS, SEQ)
        attf = att[:, :, :].rearrange("p a b -> p (a b)")
        ya = carve(attf, 0, KB, SEQ)
        og = carve(actf, 0, KB, SEQ)
        oh = carve(actf, 2048, KB, SEQ)
        resf = res[:, :, :].rearrange("p a b -> p (a b)")
        sqf = sq[:, :, :].rearrange("p a b -> p (a b)")
        q_r = carve(work, 0, 2, SEQ)
        k_r = carve(work, 512, 2, SEQ)
        rope_t = carve(work, 1024, 2, SEQ)
        vA = carve(work, 1536, 2, CW)
        iN = carve(work, 2048, 2, CW)
        p2 = carve(work, 2560, 3 * P)
        p2T = carve(work, 2944, 3 * P)
        tanh_q = carve(work, 3328, 2, SEQ)
        qh = carve(work, 3840, 2, SEQ)
        kh_s = carve(actf, 4480, 2, SEQ)
        kl = carve(resf, 0, len(LEVELS), SEQ)
        cross_e = carve(resf, 1792, 2, P)
        qx = carve(resf, 2048, P)
        dl = carve(sqf, 0, 2, SEQ)
        el = carve(sqf, 512, 2, SEQ)
        ql = carve(sqf, 1024, len(LEVELS), P)
        kx = carve(sqf, 1920, P)
        amat = carve(actf, 4096, 3, P)
        cos = carve(work, 4352, SEQ)
        sin = carve(work, 4608, SEQ)
        tanh_o = carve(actf, 4992, 2, SEQ)
        branch_t = carve(work, 0, 2, SEQ)
        head_root = carve(work, 512, 2, 4 * SEQ)
        rope_a, rope_b, rope_c = (carve(work, 3072 + SEQ * j, SEQ) for j in range(3))
        qX = carve(conv_f, 0, KB, SEQ)
        oX = carve(attf, 0, KB, SEQ)
        pX = carve(work, 0, 2, SEQ)
        pXT = carve(work, 512, 2, SEQ)
        nmax, rsum, rden, coef = (small[:, 2 * j:2 * j + 2] for j in range(4))
        neg_lam, lam_t, sub_w = small[:, 8:9], small[:, 10:14], small[:, 14:15]
        m_max, m_sum = small[0:LEAD, 16:32], small[0:LEAD, 32:48]
        lb, one_lb, lb_t = small[:, 48:56], small[:, 56:64], small[:, 64:88]
        hgrn_g = small[:, 88:96]

        table_in, res_in, mem_in, pos_in, out_sent = (sem(n) for n in ("table_in", "res_in", "mem_in", "pos_in", "out_sent"))
        landed = [sem(f"chunk_landed{s}") for s in range(RING)]
        tile_done = sem("tile_done")
        tile_read = [sem(f"tile_read{b}") for b in range(4)]
        bank_full = {b: sem(f"bank_full{b}") for b in range(2, 8)}
        bank_read = {b: sem(f"bank_read{b}") for b in range(2, 8)}
        dve_step, act_step, pool_step = sem("dve_step"), sem("act_step"), sem("pool_step")
        consts_ready = sem("consts_ready")
        squared, rooted, normed = sem("squared"), sem("rooted"), sem("normed")
        max_ready, probs_ready = sem("max_ready"), sem("probs_ready")
        kv_ready = sem("kv_ready")
        conv_ready = sem("conv_ready")
        meta_shift, meta_exp, meta_probs, meta_T, meta_done = (sem(n) for n in ("meta_shift", "meta_exp", "meta_probs", "meta_T", "meta_done"))
        att_gated = sem("att_gated")
        centered, conv_root, conv_scaled, conv_act = (sem(n) for n in ("centered", "conv_root", "conv_scaled", "conv_act"))
        mixed = sem("mixed")
        tap0, gate_act = sem("tap0"), sem("gate_act")
        act_ready = [sem("act_ready0"), sem("act_ready1")]
        forget_ready, log_ready, cum_ready, lb_exp = sem("forget_ready"), sem("log_ready"), sem("cum_ready"), sem("lb_exp")
        angle_ready, rope_ready = sem("angle_ready"), sem("rope_ready")
        diff_ready, decay_ready, level_ready, khs_ready = (sem(n) for n in ("diff_ready", "decay_ready", "level_ready", "khs_ready"))
        hgrn_ready, tanh_ready = sem("hgrn_ready"), sem("tanh_ready")
        place_waited, diff_waited = sem("place_waited"), sem("diff_waited")

        def spread(x, width):
            return x.rearrange("p (j o) -> p j o", o=1).to_broadcast([x.shape[0], x.shape[1], width])

        block = ctx.enter_context(nc.Block())

        @block.sync
        def _(sp):
            for k in range(0, KB, 2):
                sp.dma_start(res[:, k:k + 2, :], a["h_in"][:, k:k + 2, :]).then_inc(res_in, 16)
            for s in [*tile_read, *bank_full.values(), *bank_read.values(), probs_ready, level_ready, decay_ready, conv_ready, *act_ready]:
                sp.sem_inc(s, 1)
            last = [0] * RING

            def load(phase, i, c, free):
                first, _, _, _, _, slots, _, _ = STREAM.at[phase]
                hold(sp, tile_done, free)
                sp.dma_start(ring[:, slots[c], :], a["weights"][i * len(slots) + (first + c)]).then_inc(landed[slots[c]], 16)

            for phase, iters, slots, tiles in PHASES:
                ends = [sum(tiles[:c + 1]) - 1 for c in range(len(slots))]
                for c in range(len(slots)):
                    load(phase, 0, c, last[slots[c]])
                if iters > 1:
                    with sp.Fori(1, iters) as i:
                        for c in range(len(slots)):
                            load(phase, i, c, STREAM.done(phase, i - 1, ends[c]))
                for c in range(len(slots)):
                    last[slots[c]] = STREAM.done(phase, iters - 1, ends[c])
            sp.wait_ge(normed, NORMS["out"] * KB + KB)
            sp.dma_start(a["out"], xT[:, :, 0:SEQ]).then_inc(out_sent, 16)
            sp.wait_ge(out_sent, 16)

        @block.tensor
        def _(pe):
            n = Tally("tensor")

            def tile(phase, i, t, moving, width, ready=None):
                b, c, e = STREAM.bank(phase, t), t // 2, t % 2
                slot = STREAM.at[phase][5][c]
                hold(pe, tile_read[b], STREAM.before(phase, i, t))
                if e == 0:
                    pe.wait_ge(landed[slot], STREAM.landed(phase, i, c))
                for k in range(KB):
                    if ready is not None and t == 0:
                        pe.wait_ge(ready[0], ready[1] + k)
                    mm = pe.matmul(ps[:, b, 0:width], ring[:, slot, k * CW + e * P:k * CW + e * P + P], moving(k),
                                   start=k == 0, stop=k == KB - 1)
                mm.then_inc(tile_done, 1)

            def by_token(phase, i, t, first, src, extra=None):
                b, c = STREAM.bank(phase, t), t // 2
                slot = STREAM.at[phase][5][c]
                hold(pe, tile_read[b], STREAM.before(phase, i, t))
                if t % 2 == 0:
                    pe.wait_ge(landed[slot], STREAM.landed(phase, i, c))
                if extra:
                    for k in range(KB):
                        pe.matmul(ps[0:extra, b, CW:2 * CW], src(k, 0, extra), ring[:, slot, k * CW:(k + 1) * CW],
                                  start=k == 0, stop=k == KB - 1)
                for k in range(KB):
                    mm = pe.matmul(ps[:, b, 0:CW], src(k, first, P), ring[:, slot, k * CW:(k + 1) * CW],
                                   start=k == 0, stop=k == KB - 1)
                mm.then_inc(tile_done, 1)

            def channel_sum(bank, src, width, ready, order=tuple(range(KB))):
                hold(pe, bank_read[bank], n.now(bank_read[bank]))
                for k in order:
                    pe.wait_ge(ready, n.next(ready))
                    mm = pe.matmul(ps[:, bank, 0:width], ones, src[:, k, 0:width], start=k == order[0], stop=k == order[-1])
                mm.then_inc(bank_full[bank], 1)

            def norm_sum(width):
                hold(pe, rooted, n.before(rooted))
                channel_sum(4, sq, width, squared)

            pe.wait_ge(table_in, 16)
            norm_sum(T1)
            norm_sum(SEQ)

            xq = lambda k: xT[:, k, Q0:T1]
            xall = lambda k: xT[:, k, :]
            xtok = lambda k, f, m: xT[:, k, f:f + m]

            def scores1(u):
                h, i = u // 2, u % 2
                width = META + P * (i + 1)
                hold(pe, bank_read[4], n.before(bank_read[4]))
                for m in range(2):
                    mm = pe.matmul(ps[:, 4 + m, 0:width], qT[HD * m:HD * m + HD, h, LEAD + P * i:LEAD + P * i + P],
                                   kT[HD * m:HD * m + HD, h, 0:width], start=True, stop=True)
                mm.then_inc(bank_full[4], 1)

            def turn1(u):
                pe.wait_ge(probs_ready, n.next(probs_ready))
                hold(pe, bank_read[6], n.before(bank_read[6]))
                pe.transpose(ps[0:META, 6, 2 * P:3 * P], a1[:, 0:META], ident)
                for j in range(u % 2 + 1):
                    mm = pe.transpose(ps[:, 6, j * P:j * P + P], a1[:, META + j * P:META + j * P + P], ident)
                mm.then_inc(bank_full[6], 1)

            def values1(u):
                h = u // 2
                hold(pe, bank_read[6], n.now(bank_read[6]))
                hold(pe, bank_read[7], n.before(bank_read[7]))
                pe.matmul(ps[:, 7, 0:P], v_meta[0:META, h * P:h * P + P], a1M[0:META, :], start=True, stop=False)
                for j in range(u % 2 + 1):
                    mm = pe.matmul(ps[:, 7, 0:P], vN[:, j, h * P:h * P + P], a1T[:, j * P:j * P + P],
                                   start=False, stop=j == u % 2)
                mm.then_inc(bank_full[7], 1)

            pe.wait_ge(normed, KB)
            with pe.Fori(0, 4) as i:
                n.enter("heads1", i)
                for t in (0, 1):
                    tile("heads1", i, t, xq, TQ)
                for t in (2, 3):
                    tile("heads1", i, t, xall, T1)
                by_token("heads1", i, 4, META, xtok)
                by_token("heads1", i, 5, META + P, xtok, extra=META)
                pe.wait_ge(kv_ready, n.next(kv_ready))
                scores1(0)
                tile("heads1", i, 6, xall, T1)
                turn1(0)
                scores1(1)
                tile("heads1", i, 7, xall, T1)
                values1(0)
                turn1(1)
                scores1(2)
                tile("heads1", i, 8, xall, T1)
                values1(1)
                turn1(2)
                scores1(3)
                tile("heads1", i, 9, xall, T1)
                values1(2)
                turn1(3)
                values1(3)
                n.leave(4)

            for j in range(2 * HEADS):
                m, h = j // HEADS, j % HEADS
                if j == 0:
                    hold(pe, bank_read[4], n.now(bank_read[4]))
                mm = pe.matmul(ps[0:LEAD, 4 + m, h * META:(h + 1) * META], qM[HD * m:HD * m + HD, h, :],
                               kM[HD * m:HD * m + HD, h, :], start=True, stop=True)
            mm.then_inc(bank_full[4], 1)
            with pe.Fori(0, 2) as i:
                n.enter("gates1", i)
                for t in range(8):
                    tile("gates1", i, t, xq, TQ)
                n.leave(2)
            memx = lambda k: mem[:, k, :]
            memtok = lambda k, f, m: mem[:, k, f:f + m]
            pe.wait_ge(normed, 2 * KB)
            tile("mem_k", 0, 0, memx, SEQ)
            pe.wait_ge(meta_probs, 1)
            hold(pe, bank_read[6], n.now(bank_read[6]))
            for h in range(HEADS):
                mm = pe.transpose(ps[0:META, 6, LEAD * h:LEAD * h + LEAD], aM[0:LEAD, h, :], ident[0:LEAD, 0:LEAD])
            mm.then_inc(bank_full[6], 1)
            tile("mem_k", 0, 1, memx, SEQ)
            pe.wait_ge(meta_T, 1)
            hold(pe, bank_read[7], n.before(bank_read[7]))
            for h in range(HEADS):
                mm = pe.matmul(ps[:, 7, LEAD * h:LEAD * h + LEAD], vM[0:META, h * P:h * P + P], aMT[0:META, h, :],
                               start=True, stop=True)
            mm.then_inc(bank_full[7], 1)
            tile("mem_k", 0, 2, memx, SEQ)
            tile("mem_k", 0, 3, memx, SEQ)

            def head_sums(src, width, ready):
                for b in range(4, 8):
                    hold(pe, bank_read[b], n.before(bank_read[b]))
                    pe.wait_ge(ready, n.next(ready))
                    pe.matmul(ps[:, b, 0:width], ones, src(b - 4), start=True, stop=True).then_inc(bank_full[b], 1)

            head_sums(lambda j: sq[:, j, 0:TQ], TQ, squared)
            for t in (4, 5):
                tile("mem_k", 0, t, memx, SEQ)
            head_sums(lambda j: sq[:, 4 + j, 0:TQ], TQ, squared)
            for t in (6, 7):
                tile("mem_k", 0, t, memx, SEQ)
            for t in range(4):
                by_token("mem_v", 0, t, P * (t % 2), memtok)
            channel_sum(4, conv, TQ, conv_ready, (0, 2, 4, 6, 1, 3, 5, 7))
            for t in range(4, 8):
                by_token("mem_v", 0, t, P * (t % 2), memtok)
            channel_sum(5, sq, TQ, squared)
            n.before(bank_read[5])
            for t in range(8):
                tile("conv_out", 0, t, lambda k: conv[:, k, :], TQ, ready=(conv_act, 1))
            for t in range(8):
                tile("mix_out1", 0, t, lambda k: xT[:, k, 0:TQ], TQ, ready=(mixed, 1))
            norm_sum(TQ)

            def ffn(up, down, width, normed_from, reads):
                for k in range(KB):
                    pe.wait_ge(normed, normed_from + k + 1)
                x = lambda k: xT[:, k, 0:width]
                with pe.Fori(0, 5) as i:
                    n.enter(up, i)
                    for t in range(8):
                        tile(up, i, t, x, width)
                    n.leave(5)
                for t in range(4):
                    tile(up + "_end", 0, t, x, width)
                for b in range(4):
                    hold(pe, tile_read[b], STREAM.before(down + "_end", 0, b))
                for g, count in enumerate(reads):
                    pe.wait_ge(act_ready[g], count)

                def chunk(phase, i, c, first, last):
                    slot = STREAM.at[phase][5][c]
                    pe.wait_ge(landed[slot], STREAM.landed(phase, i, c))
                    kb = i * 8 + 2 * c if phase == down else 16 + 2 * c
                    for kk in range(2):
                        for t in range(KB):
                            start = first and kk == 0 and t % 2 == 0
                            mm = pe.matmul(ps[:, t // 2, t % 2 * SEQ:(t % 2 + 1) * SEQ],
                                           ring[:, slot, kk * D + t * P:kk * D + t * P + P], act[:, kb + kk, :],
                                           start=start, stop=last and kk == 1, skip_group_check=True)
                            if last and kk == 1 and t % 2 == 1:
                                mm.then_inc(tile_done, 1)
                    if not last:
                        mm.then_inc(tile_done, 1)

                for c in range(4):
                    chunk(down, 0, c, c == 0, False)
                for c in range(4):
                    chunk(down, 1, c, False, False)
                for c in range(3):
                    chunk(down + "_end", 0, c, False, c == 2)
                norm_sum(SEQ)

            ffn("up1", "down1", TQ, NORMS["ffn1"] * KB, (1 + 12, 1 + 10))

            norm_sum(SEQ)
            x2 = lambda k: xT[:, k, 0:SEQ]
            x2tok = lambda k, f, m: xT[:, k, f:f + m]
            for t in range(8):
                tile("forget", 0, t, x2, SEQ, ready=(normed, NORMS["mix2"] * KB + 1))

            def rotate(i, src, t):
                hold(pe, bank_read[2], n.before(bank_read[2]))
                for b in range(2):
                    pe.wait_ge(tile_read[b], STREAM.before("heads2", i, t + b) + 1)
                pe.matmul(ps[:, 2, :], col("rotate", 0, P), src[:, :, :].rearrange("p a b -> p (a b)"),
                          start=True, stop=True).then_inc(bank_full[2], 1)

            def scores2(j):
                s, half = j // 2, j % 2
                rows = slice(HD * half, HD * half + HD)
                if j == 0:
                    hold(pe, bank_read[2], n.now(bank_read[2]))
                hold(pe, bank_read[4], n.before(bank_read[4]))
                pe.matmul(ps[:, 4, 0:P], q_r[rows, s, 0:P], k_r[rows, s, 0:P], start=True, stop=True)
                pe.matmul(ps[:, 4, P:3 * P], q_r[rows, s, P:SEQ], k_r[rows, s, :], start=True, stop=True)\
                  .then_inc(bank_full[4], 1)

            def turn2(j):
                pe.wait_ge(probs_ready, n.next(probs_ready))
                hold(pe, bank_read[5], n.before(bank_read[5]))
                for b in range(3):
                    mm = pe.transpose(ps[:, 5, b * P:b * P + P], p2[:, b * P:b * P + P], ident)
                mm.then_inc(bank_full[5], 1)

            def values2(j):
                s, half = j // 2, j % 2
                rows = slice(HD * half, HD * half + HD)
                c = s * P + HD * half
                hold(pe, bank_read[5], n.now(bank_read[5]))
                if half == 0:
                    hold(pe, bank_read[6], n.before(bank_read[6]))
                pe.matmul(ps[rows, 6, 0:SEQ], vA[:, 0, c:c + HD], p2T[:, 0:SEQ], start=True, stop=False,
                          skip_group_check=True)
                pe.matmul(ps[rows, 6, P:SEQ], vA[:, 1, c:c + HD], p2T[:, SEQ:SEQ + P], start=False, stop=True,
                          skip_group_check=True).then_inc(bank_full[6], 1)

            def level(h, l, bank, at):
                for blk in range(2):
                    mm = pe.matmul(ps[:, bank, at + HD * blk:at + HD * blk + HD], kl[:, l, blk * P:blk * P + P],
                                   ql[:, l, blk * HD:blk * HD + HD], start=True, stop=True)
                return mm

            def hgrn_scores(h, g):
                if g == 0:
                    hold(pe, bank_read[7], n.before(bank_read[7]))
                    pe.wait_ge(khs_ready, n.next(khs_ready))
                    pe.wait_ge(level_ready, n.next(level_ready, 2))
                    for blk in range(2):
                        pe.matmul(ps[:, 7, blk * P:blk * P + P], kh_s[:, h, blk * P:blk * P + P],
                                  qh[:, h, blk * P:blk * P + P], start=True, stop=True)
                    level(h, 0, 7, 256)
                    level(h, 1, 7, 384).then_inc(bank_full[7], 1)
                elif g == 1:
                    hold(pe, bank_read[3], n.before(bank_read[3]))
                    pe.wait_ge(level_ready, n.next(level_ready, 4))
                    for l in range(2, 6):
                        mm = level(h, l, 3, (l - 2) * P)
                    mm.then_inc(bank_full[3], 1)
                else:
                    hold(pe, bank_read[7], n.before(bank_read[7]))
                    pe.wait_ge(level_ready, n.next(level_ready, 2))
                    level(h, 6, 7, 0)
                    pe.matmul(ps[:, 7, P:2 * P], kx, qx, start=True, stop=True).then_inc(bank_full[7], 1)

            def hgrn_values(h):
                hold(pe, bank_read[7], n.now(bank_read[7]))
                hold(pe, bank_read[3], n.before(bank_read[3]))
                c = h * P
                pe.matmul(ps[:, 3, 0:SEQ], iN[:, 0, c:c + P], amat[:, 0:3:2, :], start=True, stop=False,
                          skip_group_check=True)
                pe.matmul(ps[:, 3, P:SEQ], iN[:, 1, c:c + P], amat[:, 1, :], start=False, stop=True,
                          skip_group_check=True).then_inc(bank_full[3], 1)

            for b in (2, 3):
                hold(pe, tile_read[b], STREAM.before("branch_a", 0, b))
            ya_first = n.now(bank_read[6])
            with pe.Fori(0, 4) as i:
                n.enter("heads2", i)

                def proj(t):
                    if t in (2, 3, 8, 9):
                        by_token("heads2", i, t, P * (t % 2), x2tok)
                    else:
                        tile("heads2", i, t, x2, SEQ)

                for t in range(6):
                    proj(t)
                hgrn_scores(0, 0)
                proj(6)
                rotate(i, q_r, 4)
                proj(7)
                hgrn_scores(0, 1)
                rotate(i, k_r, 6)
                proj(8)
                hgrn_scores(0, 2)
                proj(9)
                scores2(0)
                hgrn_values(0)
                proj(10)
                turn2(0)
                scores2(1)
                hgrn_scores(1, 0)
                proj(11)
                values2(0)
                turn2(1)
                scores2(2)
                proj(12)
                hgrn_scores(1, 1)
                values2(1)
                turn2(2)
                scores2(3)
                proj(13)
                hgrn_scores(1, 2)
                values2(2)
                turn2(3)
                proj(14)
                hgrn_values(1)
                values2(3)
                proj(15)
                n.leave(4)

            for b in (2, 3):
                hold(pe, bank_read[b], n.now(bank_read[b]))
            for t in range(4):
                tile("branch_a", 0, t, lambda k: ya[:, k, :], SEQ, ready=(bank_read[6], ya_first + 1))
            head_sums(lambda j: sq[:, j, 0:SEQ], SEQ, squared)
            for t in range(4, 8):
                tile("branch_a", 0, t, lambda k: ya[:, k, :], SEQ)
                if t == 5:
                    head_sums(lambda j: sq[:, 4 + j, 0:SEQ], SEQ, squared)
            for t in range(8):
                tile("branch_b", 0, t, lambda k: oh[:, k, :], SEQ, ready=(hgrn_ready, 1))
            for t in range(8):
                tile("mix_out2", 0, t, x2, SEQ, ready=(mixed, KB + 1))
            norm_sum(SEQ)

            def scores_x(h):
                hold(pe, bank_read[4], n.before(bank_read[4]))
                t = 2 * h + 1
                b = STREAM.bank("cross_q", t)
                pe.wait_ge(tile_read[b], STREAM.before("cross_q", 0, t) + 1)
                for blk in range(2):
                    for e in range(2):
                        mm = pe.matmul(ps[:, 4, blk * SEQ:(blk + 1) * SEQ], qX[:, 2 * h + e, blk * P:blk * P + P],
                                       k_mem[:, 2 * h + e, :], start=e == 0, stop=e == 1)
                mm.then_inc(bank_full[4], 1)

            def turn_x(h):
                pe.wait_ge(probs_ready, n.next(probs_ready))
                hold(pe, bank_read[5], n.before(bank_read[5]))
                for m in range(2):
                    for blk in range(2):
                        mm = pe.transpose(ps[:, 5, m * SEQ + blk * P:m * SEQ + blk * P + P],
                                          pX[:, blk, m * P:m * P + P], ident)
                mm.then_inc(bank_full[5], 1)

            def values_x(h):
                hold(pe, bank_read[5], n.now(bank_read[5]))
                hold(pe, bank_read[6], n.before(bank_read[6]))
                for e in range(2):
                    for m in range(2):
                        c = h * SEQ + e * P
                        mm = pe.matmul(ps[:, 6, e * SEQ:(e + 1) * SEQ], v_mem[:, m, c:c + P], pXT[:, m, :],
                                       start=m == 0, stop=m == 1)
                mm.then_inc(bank_full[6], 1)

            for h in range(4):
                tile("cross_q", 0, 2 * h, x2, SEQ, ready=(normed, NORMS["cross"] * KB + 1))
                tile("cross_q", 0, 2 * h + 1, x2, SEQ)
                if h >= 1:
                    scores_x(h - 1)
                if h >= 2:
                    turn_x(h - 2)
                    values_x(h - 2)
            turn_x(2)
            scores_x(3)
            values_x(2)
            turn_x(3)
            values_x(3)
            hold(pe, bank_read[6], n.now(bank_read[6]))
            for t in range(8):
                tile("cross_out", 0, t, lambda k: oX[:, k, :], SEQ)
            norm_sum(SEQ)
            ffn("up2", "down2", SEQ, NORMS["ffn2"] * KB, ())

        @block.scalar
        def _(sc):
            n = Tally("scalar")

            def act_fn(out, src, fn, sem_, **kw):
                ins = sc.activation(out, src, fn, **kw)
                ins.then_inc(sem_, 1)
                n.before(sem_)
                return ins

            def copy_tile(phase, i, t, out, src, scale=1.0, fn=ACT.Copy):
                b = STREAM.bank(phase, t)
                sc.wait_ge(tile_done, STREAM.done(phase, i, t))
                sc.activation(out, src, fn, scale=scale).then_inc(tile_read[b], 1)

            def root_of_mean(bank, width, count, eps, out, sem_):
                sc.wait_ge(bank_full[bank], n.next(bank_full[bank]))
                sc.activation(out, ps[:, bank, 0:width], ACT.Sqrt, bias=col(eps), scale=1.0 / count).then_inc(sem_, 1)

            sc.dma_start(table[:, :], a["table"]).then_inc(table_in, 16)
            sc.dma_start(mem[:, :, :], a["mem"]).then_inc(mem_in, 16)
            sc.dma_start(pos_i, a["positions"]).then_inc(pos_in, 16)
            sc.wait_ge(res_in, 64)
            sc.wait_ge(table_in, 16)
            for k in range(KB):
                act_fn(sq[:, k, :], res[:, k, :], ACT.Square, squared)
            root_of_mean(4, T1, D, "eps6", root[:, :], rooted)
            sc.wait_ge(mem_in, 16)
            for k in range(KB):
                act_fn(sq[:, k, 0:SEQ], mem[:, k, :], ACT.Square, squared)
            sc.wait_ge(normed, KB)
            root_of_mean(4, SEQ, D, "eps6", root[:, 0:SEQ], rooted)
            sc.wait_ge(consts_ready, 1)
            sc.activation(lam_t[:, 2:4], lam_t[:, 0:2], ACT.Exp).then_inc(lb_exp, 1)

            def exps1(u):
                width = META + P * (u % 2 + 1)
                sc.wait_ge(max_ready, n.next(max_ready))
                hold(sc, probs_ready, n.before(probs_ready))
                for m in range(2):
                    ins = sc.activation(E1[:, m, 0:width], ps[:, 4 + m, 0:width], ACT.Exp, bias=nmax[:, m:m + 1],
                                        accum_out=rsum[:, m:m + 1])
                ins.then_inc(bank_read[4], 1)

            def turned1(u):
                sc.wait_ge(bank_full[6], n.next(bank_full[6]))
                hold(sc, bank_full[7], n.now(bank_full[7]))
                sc.activation(a1M[0:META, :], ps[0:META, 6, 2 * P:3 * P], ACT.Copy)
                sc.activation(a1T[:, 0:P * (u % 2 + 1)], ps[:, 6, 0:P * (u % 2 + 1)], ACT.Copy).then_inc(bank_read[6], 1)

            def output1(i, u):
                h = u // 2
                sc.wait_ge(bank_full[7], n.next(bank_full[7]))
                sc.activation(att[:, i * 2 + h, LEAD + P * (u % 2):LEAD + P * (u % 2) + P], ps[:, 7, 0:P],
                              ACT.Copy).then_inc(bank_read[7], 1)

            sc.wait_ge(normed, KB)
            with sc.Fori(0, 4) as i:
                n.enter("heads1", i)
                hold(sc, bank_full[4], n.before(bank_full[4], 4))
                for t in (0, 1):
                    copy_tile("heads1", i, t, qT[:, t, :], ps[:, STREAM.bank("heads1", t), 0:TQ], HD ** -0.5)
                for t in (2, 3):
                    copy_tile("heads1", i, t, kT[:, t - 2, :], ps[:, STREAM.bank("heads1", t), 0:T1])
                hold(sc, bank_full[7], n.now(bank_full[7]))
                copy_tile("heads1", i, 4, vN[:, 0, :], ps[:, STREAM.bank("heads1", 4), 0:CW])
                sc.wait_ge(tile_done, STREAM.done("heads1", i, 5))
                bk = STREAM.bank("heads1", 5)
                sc.activation(v_meta[0:META, :], ps[0:META, bk, CW:2 * CW], ACT.Copy)
                sc.activation(vM[0:META, bass.ds(i * CW, CW)], ps[0:META, bk, CW:2 * CW], ACT.Copy)
                sc.activation(vN[:, 1, :], ps[:, bk, 0:CW], ACT.Copy).then_inc(tile_read[bk], 1)
                for t in range(4):
                    sc.wait_ge(tile_read[STREAM.bank("heads1", t)], STREAM.before("heads1", i, t) + 1)
                sc.activation(qM[:, bass.ds(i * 2, 2), :], qT[:, :, 0:LEAD], ACT.Copy)
                sc.activation(kM[:, bass.ds(i * 2, 2), :], kT[:, :, 0:META], ACT.Copy).then_inc(kv_ready, 1)
                exps1(0)
                for u in range(1, 4):
                    if u < 3:
                        bk = STREAM.bank("heads1", 5 + u)
                        sc.wait_ge(tile_done, STREAM.done("heads1", i, 5 + u))
                        bu = STREAM.bank("heads1", 7 + u)
                        hold(sc, tile_read[bu], STREAM.before("heads1", i, 7 + u))
                        sc.activation(tanh_b[:, u - 1, :], ps[:, bk, 0:T1], ACT.Tanh, scale=0.5).then_inc(tile_read[bk], 1)
                    turned1(u - 1)
                    if u >= 2:
                        output1(i, u - 2)
                    exps1(u)
                turned1(3)
                output1(i, 2)
                output1(i, 3)
                n.leave(4)
            with sc.Fori(0, 2) as i:
                n.enter("gates1", i)
                for t in range(8):
                    bk = STREAM.bank("gates1", t)
                    sc.wait_ge(tile_done, STREAM.done("gates1", i, t))
                    sc.activation(gates[:, i * 8 + t, :], ps[:, bk, 0:TQ], ACT.Tanh, scale=0.5).then_inc(tile_read[bk], 1)
                n.leave(2)
            sc.wait_ge(meta_shift, 2)
            sc.activation(sM[0:LEAD, :, :], sM[0:LEAD, :, :], ACT.Exp).then_inc(meta_exp, 1)

            def mem_k(t):
                copy_tile("mem_k", 0, t, k_mem[:, t, :], ps[:, STREAM.bank("mem_k", t), 0:SEQ])

            mem_k(0)
            sc.wait_ge(bank_full[6], n.next(bank_full[6]))
            sc.activation(aMT[0:META, :, :], ps[0:META, 6, 0:LEAD * HEADS].rearrange("p (h q) -> p h q", q=LEAD),
                          ACT.Copy).then_inc(meta_T, 1)
            mem_k(1)
            sc.wait_ge(bank_full[7], n.next(bank_full[7]))
            sc.activation(att[:, :, 0:LEAD], ps[:, 7, 0:LEAD * HEADS].rearrange("p (h q) -> p h q", q=LEAD),
                          ACT.Copy).then_inc(bank_read[7], 1)
            sc.wait_ge(bank_read[7], 1 + 4 * 4 + 1)
            for h in range(4):
                act_fn(sq[:, h, 0:TQ], att[:, h, :], ACT.Square, squared)
            mem_k(2)
            mem_k(3)
            for h in range(4):
                act_fn(sq[:, 4 + h, 0:TQ], att[:, 4 + h, :], ACT.Square, squared)
            n.next(bank_full[4])
            for g in range(2):
                for j in range(4):
                    root_of_mean(4 + j, TQ, P, "eps6", att_root[:, g, j * TQ:(j + 1) * TQ], bank_read[4 + j])
                mem_k(4 + 2 * g)
                mem_k(5 + 2 * g)
            for t in range(8):
                for k in range(2 * t - 8, max(2 * t - 6, 0)):
                    if k >= 0:
                        sc.wait_ge(centered, k + 1)
                        act_fn(sq[:, k, 0:TQ], conv[:, k, :], ACT.Square, squared)
                copy_tile("mem_v", 0, t, v_mem[:, t % 2, t // 2 * CW:(t // 2 + 1) * CW],
                          ps[:, STREAM.bank("mem_v", t), 0:CW])
            n.next(bank_full[4])
            root_of_mean(5, TQ, D, "eps5", root[:, 0:TQ], bank_read[5])
            for k in range(KB):
                sc.wait_ge(conv_scaled, k + 1)
                sc.activation(conv[:, k, :], conv[:, k, :], ACT.Silu, scale=col("conv_ln_w", k),
                              bias=col("conv_ln_b", k)).then_inc(conv_act, 1)

            def squares_of_sum(phase, src):
                for t in range(KB):
                    b = STREAM.bank(phase, t)
                    sc.wait_ge(tile_read[b], STREAM.before(phase, 0, t) + 1)
                    act_fn(sq[:, t, 0:src(t).shape[-1]], src(t), ACT.Square, squared)

            squares_of_sum("mix_out1", lambda t: res[:, t, Q0:T1])
            root_of_mean(4, TQ, D, "eps6", root[:, 0:TQ], rooted)

            def ffn_taps(up, weights):
                def group(phase, i, j, g):
                    hold(sc, act_ready[g % 2], n.before(act_ready[g % 2], 2))
                    for e in range(4):
                        t = 4 * (g % 2) * (phase == up) + e
                        w = j + e if e < 2 else j + (FT + e - 2)
                        bk = STREAM.bank(phase, t)
                        sc.wait_ge(tile_done, STREAM.done(phase, i, t))
                        act_fn(taps[:, 4 * (g % 2) + e, :], ps[:, bk, 0:SEQ], ACT.Identity, tap0,
                               scale=table[:, bass.ds(w * 3 + AT["ffn_dw_w"], 1)] if not isinstance(w, int) else col("ffn_dw_w", 3 * w),
                               bias=table[:, bass.ds(w + AT["ffn_dw_b"], 1)] if not isinstance(w, int) else col("ffn_dw_b", w))
                        if e == 1:
                            for x in range(2):
                                tx = 4 * (g % 2) * (phase == up) + x
                                sc.wait_ge(tile_read[STREAM.bank(phase, tx)], STREAM.before(phase, i, tx) + 1)
                                act_fn(silu_g[:, 2 * (g % 2) + x, :], taps[:, 4 * (g % 2) + x, :], ACT.Silu, gate_act)
                return group

            group = ffn_taps("up1", None)
            with sc.Fori(0, 5) as i:
                n.enter("up1", i)
                group("up1", i, i * 4, 0)
                group("up1", i, i * 4 + 2, 1)
                n.leave(5)
            group("up1_end", 0, 20, 0)

            def squares_after_down(down, src):
                for t in range(KB):
                    sc.wait_ge(tile_read[t // 2], STREAM.before(down + "_end", 0, t // 2) + 1)
                    act_fn(sq[:, t, 0:SEQ], src(t), ACT.Square, squared)

            for k in range(2):
                sc.wait_ge(angle_ready, k + 1)
                sc.activation((sin, cos)[k], (sin, cos)[k], ACT.Sin).then_inc(rope_ready, 1)
            sc.wait_ge(consts_ready, 2)
            sc.activation(lb_t[:, 0:16], lb_t[:, 0:16], ACT.Exp).then_inc(lb_exp, 1)
            squares_after_down("down1", lambda t: res[:, t, META:T1])
            root_of_mean(4, SEQ, D, "eps6", root[:, 0:SEQ], rooted)
            for k in range(KB):
                sc.wait_ge(normed, NORMS["final1"] * KB + k + 1)
                act_fn(sq[:, k, 0:SEQ], res2[:, k, :], ACT.Square, squared)
            root_of_mean(4, SEQ, D, "eps6", root[:, 0:SEQ], rooted)
            for t in range(KB):
                copy_tile("forget", 0, t, bT[:, t, :], ps[:, STREAM.bank("forget", t), 0:SEQ], fn=ACT.Sigmoid)
            sc.wait_ge(forget_ready, KB)
            sc.activation(conv_f[:, 0:KB * SEQ], conv_f[:, 0:KB * SEQ], ACT.Ln).then_inc(log_ready, 1)

            def reuse(x):
                hold(sc, level_ready, n.now(level_ready) - (x != 0))
                n.before(level_ready)

            def decay(x):
                sc.wait_ge(diff_ready, n.next(diff_ready))
                reuse(x)
                sc.activation(el[:, x % 2, :], dl[:, x % 2, :], ACT.Exp).then_inc(decay_ready, 1)

            def cross_decay(i, h):
                bh = bT[:, i * 2 + h, :]
                reuse(1)
                sc.activation(cross_e[:, 0, :], bh[:, 0:P], ACT.Exp, scale=-1.0, bias=bh[:, P - 1:P])
                sc.activation(cross_e[:, 1, :], bh[:, P:SEQ], ACT.Exp).then_inc(decay_ready, 1)

            def head_keys(i, h):
                sc.activation(kh_s[:, h, :], kh[:, i * 2 + h, :], ACT.Copy).then_inc(khs_ready, 1)

            def exps2(j):
                sc.wait_ge(max_ready, n.next(max_ready, 2))
                sc.activation(p2[:, 0:P], ps[:, 4, 0:P], ACT.Exp, bias=nmax[:, 0:1], accum_out=rsum[:, 0:1])
                sc.activation(p2[:, P:3 * P], ps[:, 4, P:3 * P], ACT.Exp, bias=nmax[:, 1:2],
                              accum_out=rsum[:, 1:2]).then_inc(bank_read[4], 1)

            def turned2():
                sc.wait_ge(bank_full[5], n.next(bank_full[5]))
                hold(sc, bank_full[6], n.now(bank_full[6]))
                sc.activation(p2T, ps[:, 5, 0:3 * P], ACT.Copy).then_inc(bank_read[5], 1)
                n.next(bank_full[6])

            def output2(i, s):
                sc.wait_ge(bank_full[6], n.now(bank_full[6]))
                sc.activation(ya[:, i * 2 + s, :], ps[:, 6, 0:SEQ], ACT.Copy).then_inc(bank_read[6], 1)

            def hgrn_output(i, h):
                n.next(bank_full[3])
                sc.wait_ge(bank_full[3], n.next(bank_full[3]))
                sc.activation(oh[:, i * 2 + h, :], ps[:, 3, 0:SEQ], ACT.Copy).then_inc(bank_read[3], 1)

            sc.wait_ge(cum_ready, HEADS)
            with sc.Fori(0, 4) as i:
                n.enter("heads2", i)

                def copy2(t, out, width=SEQ, **kw):
                    copy_tile("heads2", i, t, out, ps[:, STREAM.bank("heads2", t), 0:width], **kw)

                def tanh2(t, out, sem_):
                    sc.wait_ge(tile_done, STREAM.done("heads2", i, t))
                    sc.activation(out, ps[:, STREAM.bank("heads2", t), 0:SEQ], ACT.Tanh, scale=0.5).then_inc(sem_, 1)

                tanh2(0, tanh_q[:, 0, :], tanh_ready)
                tanh2(1, tanh_q[:, 1, :], tanh_ready)
                hold(sc, bank_full[7], n.before(bank_full[7], 4))
                decay(0)
                decay(1)
                hold(sc, bank_full[3], n.now(bank_full[3]))
                copy2(2, iN[:, 0, :])
                copy2(3, iN[:, 1, :])
                head_keys(i, 0)
                head_keys(i, 1)
                decay(2)
                decay(3)
                hold(sc, bank_full[4], n.before(bank_full[4], 4))
                copy2(4, q_r[:, 0, :], scale=HD ** -0.5)
                copy2(5, q_r[:, 1, :], scale=HD ** -0.5)
                decay(4)
                decay(5)
                copy2(6, k_r[:, 0, :])
                copy2(7, k_r[:, 1, :])
                decay(6)
                cross_decay(i, 0)
                hold(sc, bank_full[6], n.now(bank_full[6]))
                copy2(8, vA[:, 0, :])
                copy2(9, vA[:, 1, :])
                exps2(0)
                decay(7)
                decay(8)
                hgrn_output(i, 0)
                copy2(10, gates[:, i * 2, 0:SEQ], fn=ACT.Tanh, scale=0.5)
                turned2()
                exps2(1)
                for x in range(9, 13):
                    decay(x)
                copy2(11, gates[:, i * 2 + 1, 0:SEQ], fn=ACT.Tanh, scale=0.5)
                turned2()
                exps2(2)
                decay(13)
                cross_decay(i, 1)
                copy2(12, gates[:, i * 2 + KB, 0:SEQ], fn=ACT.Tanh, scale=0.5)
                output2(i, 0)
                turned2()
                exps2(3)
                copy2(13, gates[:, i * 2 + KB + 1, 0:SEQ], fn=ACT.Tanh, scale=0.5)
                turned2()
                tanh2(14, tanh_o[:, 0, :], tanh_ready)
                hgrn_output(i, 1)
                output2(i, 1)
                tanh2(15, tanh_o[:, 1, :], tanh_ready)
                n.leave(4)
            sc.wait_ge(bank_read[3], 1 + 2 * HEADS)
            for h in range(HEADS):
                act_fn(sq[:, h, 0:SEQ], oh[:, h, :], ACT.Square, squared)
            for g in range(2):
                for j in range(4):
                    root_of_mean(4 + j, SEQ, P, "eps6", head_root[:, g, j * SEQ:(j + 1) * SEQ], bank_read[4 + j])
            squares_of_sum("mix_out2", lambda t: res2[:, t, :])
            root_of_mean(4, SEQ, D, "eps6", root[:, 0:SEQ], rooted)

            def exps_x(h):
                sc.wait_ge(max_ready, n.next(max_ready))
                for blk in range(2):
                    ins = sc.activation(pX[:, blk, :], ps[:, 4, blk * SEQ:(blk + 1) * SEQ], ACT.Exp,
                                        bias=nmax[:, blk:blk + 1], accum_out=rsum[:, blk:blk + 1])
                ins.then_inc(bank_read[4], 1)

            def turned_x(h):
                sc.wait_ge(bank_full[5], n.next(bank_full[5]))
                hold(sc, bank_full[6], n.now(bank_full[6]))
                sc.activation(pXT.rearrange("p a b -> p (a b)"), ps[:, 5, :], ACT.Copy).then_inc(bank_read[5], 1)

            def output_x(h):
                sc.wait_ge(bank_full[6], n.next(bank_full[6]))
                sc.activation(oX[:, 2 * h:2 * h + 2, :], ps[:, 6, :].rearrange("p (e t) -> p e t", t=SEQ), ACT.Copy)\
                  .then_inc(bank_read[6], 1)

            def query_x(h):
                for t in (2 * h, 2 * h + 1):
                    copy_tile("cross_q", 0, t, qX[:, t, :], ps[:, STREAM.bank("cross_q", t), 0:SEQ], SEQ ** -0.5)

            query_x(0)
            query_x(1)
            exps_x(0)
            query_x(2)
            turned_x(0)
            exps_x(1)
            output_x(0)
            query_x(3)
            turned_x(1)
            exps_x(2)
            output_x(1)
            turned_x(2)
            exps_x(3)
            output_x(2)
            turned_x(3)
            output_x(3)
            n.next(bank_full[4], 4)
            squares_of_sum("cross_out", lambda t: res2[:, t, :])
            root_of_mean(4, SEQ, D, "eps6", root[:, 0:SEQ], rooted)

            def gates2(phase, i, g):
                for x in range(2):
                    t = 4 * (g % 2) * (phase == "up2") + x
                    bv = STREAM.bank(phase, t + 2)
                    hold(sc, tile_read[bv], STREAM.before(phase, i, t + 2))
                    b = STREAM.bank(phase, t)
                    sc.wait_ge(tile_done, STREAM.done(phase, i, t))
                    sc.activation(silu_g[:, 2 * (g % 2) + x, :], ps[:, b, 0:SEQ], ACT.Silu).then_inc(tile_read[b], 1)

            with sc.Fori(0, 5) as i:
                n.enter("up2", i)
                gates2("up2", i, 0)
                gates2("up2", i, 1)
                n.leave(5)
            gates2("up2_end", 0, 0)
            squares_after_down("down2", lambda t: res2[:, t, :])
            root_of_mean(4, SEQ, D, "eps6", root[:, 0:SEQ], rooted)

        @block.vector
        def _(ve):
            n = Tally("vector")

            def step(ins):
                ins.then_inc(dve_step, 1)
                ve.wait_ge(dve_step, n.next(dve_step))

            def norm(width, src, dst, weight, roots):
                ve.wait_ge(rooted, roots)
                step(ve.reciprocal(rinv[:, 0:width], root[:, 0:width]))
                for k in range(KB):
                    ve.scalar_tensor_tensor(dst(k), src(k), col(weight, k), rinv[:, 0:width], ALU.mult, ALU.mult)\
                      .then_inc(normed, 1)

            ve.wait_ge(table_in, 16)
            ve.memset(glu[:, :, 0:TAPS - 1], 0.0)
            norm(T1, lambda k: res[:, k, :], lambda k: xT[:, k, :], "norm_mix_w", 1)
            lam = col("lambdas", 0, 4 * HD)
            step(ve.tensor_tensor(lam[:, 0:HD], lam[:, 0:HD], lam[:, HD:2 * HD], ALU.mult))
            step(ve.tensor_tensor(lam[:, 2 * HD:3 * HD], lam[:, 2 * HD:3 * HD], lam[:, 3 * HD:4 * HD], ALU.mult))
            step(ve.reduce_sum(lam_t[:, 0:1], lam[:, 0:HD], AX))
            ve.reduce_sum(lam_t[:, 1:2], lam[:, 2 * HD:3 * HD], AX).then_inc(consts_ready, 1)
            cw = col("conv_dw_w", 0, KB * TAPS)
            step(ve.tensor_scalar(cw, cw, 0.5, None, ALU.mult))
            step(ve.tensor_scalar(sub_w, col("subln_w"), 1.0 - LAMBDA_INIT, None, ALU.mult))
            norm(SEQ, lambda k: mem[:, k, :], lambda k: mem[:, k, :], "norm_mem_g_2", 2)
            ve.wait_ge(lb_exp, 1)
            step(ve.tensor_tensor(neg_lam, lam_t[:, 3:4], lam_t[:, 2:3], ALU.subtract))
            step(ve.tensor_scalar(neg_lam, neg_lam, -LAMBDA_INIT, None, ALU.add))

            def maxima1(u):
                width = META + P * (u % 2 + 1)
                ve.wait_ge(bank_full[4], n.next(bank_full[4]))
                step(ve.memset(ps[0:CHUNK, 4:6, width - CHUNK:width], NEG))
                ve.tensor_reduce(nmax, ps[:, 4:6, 0:width], AX, ALU.max, negate=True).then_inc(max_ready, 1)

            def combine1(u):
                width = META + P * (u % 2 + 1)
                ve.wait_ge(bank_read[4], n.next(bank_read[4]))
                step(ve.reciprocal(rden, rsum))
                step(ve.tensor_tensor(coef[:, 0:1], rden[:, 1:2], neg_lam, ALU.mult))
                hold(ve, bank_full[6], n.before(bank_full[6]))
                step(ve.tensor_scalar(a1[:, 0:width], E1[:, 0, 0:width], rden[:, 0:1], None, ALU.mult))
                ve.scalar_tensor_tensor(a1[:, 0:width], E1[:, 1, 0:width], coef[:, 0:1], a1[:, 0:width],
                                        ALU.mult, ALU.add).then_inc(probs_ready, 1)

            def glu1(i, h):
                b, g = STREAM.bank("heads1", 8 + h), STREAM.bank("heads1", 6 + h)
                ve.wait_ge(tile_read[g], STREAM.before("heads1", i, 6 + h) + 1)
                ve.wait_ge(tile_done, STREAM.done("heads1", i, 8 + h))
                ve.scalar_tensor_tensor(glu[:, i * 2 + h, TAPS - 1:TAPS - 1 + T1], tanh_b[:, h, :], 1.0,
                                        ps[:, b, 0:T1], ALU.add, ALU.mult).then_inc(tile_read[b], 1)

            def conv1(j):
                def w(k):
                    return table[:, bass.ds(j * TAPS + (AT["conv_dw_w"] + k), 1)]

                def u(k):
                    return glu[:, j, Q0 + k:Q0 + k + TQ]

                hold(ve, conv_ready, n.before(conv_ready))
                sums = [conv[:, j, :], conv_odd]
                ve.tensor_scalar(sums[0], u(0), w(0), table[:, bass.ds(j + AT["conv_dw_b"], 1)], ALU.mult, ALU.add)\
                  .then_inc(dve_step, 1)
                n.next(dve_step)
                ve.tensor_scalar(sums[1], u(1), w(1), None, ALU.mult).then_inc(dve_step, 1)
                for k in range(2, TAPS):
                    ve.wait_ge(dve_step, n.now(dve_step))
                    ve.scalar_tensor_tensor(sums[k % 2], u(k), w(k), sums[k % 2], ALU.mult, ALU.add).then_inc(dve_step, 1)
                    n.next(dve_step)
                ve.wait_ge(dve_step, n.next(dve_step))
                ve.tensor_tensor(sums[0], sums[0], sums[1], ALU.add).then_inc(conv_ready, 1)

            n.next(bank_full[4], 2)
            with ve.Fori(0, 4) as i:
                n.enter("heads1", i)
                maxima1(0)
                combine1(0)
                maxima1(1)
                combine1(1)
                maxima1(2)
                combine1(2)
                glu1(i, 0)
                maxima1(3)
                combine1(3)
                glu1(i, 1)
                ve.wait_ge(tile_read[STREAM.bank("heads1", 9)], STREAM.before("heads1", i, 9) + 1)
                conv1(i * 2)
                n.leave(4)

            ve.wait_ge(bank_full[4], n.next(bank_full[4]))
            for m in range(2):
                s_m = ps[0:LEAD, 4 + m, 0:HEADS * META].rearrange("p (h k) -> p h k", k=META)
                top = m_max[:, m * HEADS:(m + 1) * HEADS]
                step(ve.tensor_reduce(top, s_m, AX, ALU.max))
                ve.tensor_tensor(sM[0:LEAD, m * HEADS:(m + 1) * HEADS, :], s_m, spread(top, META), ALU.subtract)\
                  .then_inc(meta_shift, 1)
            with ve.Fori(0, 2) as i:
                n.enter("conv odd a", i)
                conv1(i * 2 + 1)
                n.leave(2)
            ve.wait_ge(meta_exp, 1)
            step(ve.reduce_sum(m_sum, sM[0:LEAD, :, :], AX))
            step(ve.reciprocal(m_sum, m_sum))
            step(ve.tensor_tensor(sM[0:LEAD, :, :], sM[0:LEAD, :, :], spread(m_sum, META), ALU.mult))
            ve.scalar_tensor_tensor(aM[0:LEAD, :, :], sM[0:LEAD, HEADS:, :], neg_lam[0:LEAD, :], sM[0:LEAD, 0:HEADS, :],
                                    ALU.mult, ALU.add).then_inc(meta_probs, 1)
            with ve.Fori(0, 2) as i:
                n.enter("conv odd b", i)
                conv1(i * 2 + 5)
                n.leave(2)
            ve.wait_ge(bank_full[4], n.next(bank_full[4], 3))
            for k in range(KB):
                ve.scalar_tensor_tensor(conv[:, k, :], ps[:, 4, 0:TQ], -1.0 / D, conv[:, k, :], ALU.mult, ALU.add)\
                  .then_inc(centered, 1)
            ve.wait_ge(bank_read[7], 1 + 4 * 4 + 1 + 2)
            for g in range(2):
                heads = att[:, 4 * g:4 * g + 4, :].rearrange("p h t -> p (h t)")
                r_g = att_root[:, g, :]
                step(ve.reciprocal(r_g, r_g))
                step(ve.scalar_tensor_tensor(heads, heads, sub_w, r_g, ALU.mult, ALU.mult))
                ve.scalar_tensor_tensor(heads, gates[:, 4 * g:4 * g + 4, :].rearrange("p h t -> p (h t)"), 1.0, heads,
                                        ALU.add, ALU.mult).then_inc(att_gated, 1)
            ve.wait_ge(bank_read[5], 1 + 2 + 1)
            step(ve.reciprocal(rinv[:, 0:TQ], root[:, 0:TQ]))
            for k in range(KB):
                ve.tensor_tensor(conv[:, k, :], conv[:, k, :], rinv[:, 0:TQ], ALU.mult).then_inc(conv_scaled, 1)
            ve.wait_ge(att_gated, 2)
            for t in range(KB):
                b = STREAM.bank("conv_out", t)
                ve.wait_ge(tile_done, STREAM.done("conv_out", 0, t))
                ve.scalar_tensor_tensor(xT[:, t, 0:TQ], gates[:, KB + t, :], 1.0, ps[:, b, 0:TQ], ALU.add, ALU.mult)\
                  .then_inc(tile_read[b], 1)
                ve.wait_ge(tile_read[b], STREAM.before("conv_out", 0, t) + 1)
                ve.tensor_tensor(xT[:, t, 0:TQ], xT[:, t, 0:TQ], att[:, t, :], ALU.add).then_inc(mixed, 1)

            def add_tiles(phase, dst, width):
                for t in range(KB):
                    b = STREAM.bank(phase, t)
                    ve.wait_ge(tile_done, STREAM.done(phase, 0, t))
                    ve.scalar_tensor_tensor(dst(t), ps[:, b, 0:width], HALF[phase], dst(t), ALU.mult, ALU.add)\
                      .then_inc(tile_read[b], 1)

            HALF = {"mix_out1": 0.5, "mix_out2": 0.5, "cross_out": 1.0}
            add_tiles("mix_out1", lambda t: res[:, t, Q0:T1], TQ)
            norm(TQ, lambda k: res[:, k, Q0:T1], lambda k: xT[:, k, 0:TQ], "norm_ffn_w", 3)

            def group1(phase, i, j, g):
                for e in range(4):
                    t = 4 * (g % 2) * (phase == "up1") + e
                    w = j + e if e < 2 else j + (FT + e - 2)
                    b = STREAM.bank(phase, t)
                    acc = taps[:, 4 * (g % 2) + e, :]

                    def tap(k):
                        return table[:, bass.ds(w * 3 + (AT["ffn_dw_w"] + k), 1)] if not isinstance(w, int) else \
                            col("ffn_dw_w", 3 * w + k)

                    ve.wait_ge(tap0, n.next(tap0))
                    step(ve.scalar_tensor_tensor(acc, ps[:, b, 1:SEQ + 1], tap(1), acc, ALU.mult, ALU.add))
                    ve.scalar_tensor_tensor(acc, ps[:, b, 2:SEQ + 2], tap(2), acc, ALU.mult, ALU.add)\
                      .then_inc(tile_read[b], 1)
                    if e >= 2:
                        ve.wait_ge(tile_read[b], STREAM.before(phase, i, t) + 1)
                        ve.wait_ge(gate_act, n.next(gate_act))
                        ve.tensor_tensor(act[:, j + (e - 2), :], silu_g[:, 2 * (g % 2) + e - 2, :], acc, ALU.mult)\
                          .then_inc(act_ready[g % 2], 1)

            with ve.Fori(0, 5) as i:
                n.enter("up1", i)
                group1("up1", i, i * 4, 0)
                group1("up1", i, i * 4 + 2, 1)
                n.leave(5)
            group1("up1_end", 0, 20, 0)

            def add_down(down, dst):
                for b in range(4):
                    ve.wait_ge(tile_done, STREAM.done(down + "_end", 0, 2 + b))
                    ve.tensor_tensor(dst(b), ps[:, b, :].rearrange("p (t s) -> p t s", s=SEQ), dst(b), ALU.add)\
                      .then_inc(tile_read[b], 1)


            ve.wait_ge(pos_in, 16)
            ang, turns, over = rope_a, rope_b, rope_c
            step(ve.tensor_copy(turns, pos_i))
            step(ve.tensor_scalar(ang, turns, col("inv_freq"), None, ALU.mult))
            step(ve.tensor_scalar(turns, ang, 0.15915494309189535, MAGIC, ALU.mult, ALU.add))
            step(ve.tensor_scalar(turns, turns, -MAGIC, None, ALU.add))
            for part in TWO_PI:
                step(ve.scalar_tensor_tensor(ang, turns, -part, ang, ALU.mult, ALU.add))
            ve.tensor_scalar(sin, ang, -PI_IN, PI_IN, ALU.max, ALU.min).then_inc(angle_ready, 1)
            step(ve.tensor_scalar(ang, ang, 1.5707963267948966, None, ALU.add))
            step(ve.tensor_scalar(over, ang, 3.141592653589793, -6.283185307179586, ALU.is_gt, ALU.mult))
            step(ve.tensor_tensor(ang, ang, over, ALU.add))
            ve.tensor_scalar(cos, ang, -PI_IN, PI_IN, ALU.max, ALU.min).then_inc(angle_ready, 1)
            l0, l1 = col("lb_logits", 0, KB), col("lb_logits", KB, KB)
            step(ve.tensor_tensor(lb_t[:, 16:24], l0, l1, ALU.max))
            ve.tensor_tensor(lb_t[:, 0:8], l0, lb_t[:, 16:24], ALU.subtract)
            ve.tensor_tensor(lb_t[:, 8:16], l1, lb_t[:, 16:24], ALU.subtract).then_inc(consts_ready, 1)
            ve.wait_ge(lb_exp, 2)
            step(ve.tensor_tensor(lb_t[:, 16:24], lb_t[:, 0:8], lb_t[:, 8:16], ALU.add))
            step(ve.reciprocal(lb_t[:, 16:24], lb_t[:, 16:24]))
            step(ve.tensor_tensor(lb, lb_t[:, 0:8], lb_t[:, 16:24], ALU.mult))
            step(ve.tensor_scalar(one_lb, lb, -1.0, 1.0, ALU.mult, ALU.add))
            step(ve.tensor_scalar(hgrn_g, col("hgrn_norm_g_2", 0, KB), 0.5, None, ALU.mult))

            add_down("down1", lambda b: res[:, 2 * b:2 * b + 2, META:T1])
            norm(SEQ, lambda k: res[:, k, META:T1], lambda k: res2[:, k, :], "norm_final_w", 4)

            norm(SEQ, lambda k: res2[:, k, :], lambda k: xT[:, k, 0:SEQ], "norm_mix_g_2", 5)
            for t in range(KB):
                b = STREAM.bank("forget", t)
                ve.wait_ge(tile_read[b], STREAM.before("forget", 0, t) + 1)
                step(ve.tensor_scalar(bT[:, t, :], bT[:, t, :], one_lb[:, t:t + 1], lb[:, t:t + 1], ALU.mult, ALU.add))
                step(ve.tensor_scalar(kh[:, t, :], bT[:, t, :], -KEY_SCALE, KEY_SCALE, ALU.mult, ALU.add))
                ve.tensor_scalar(bT[:, t, :], bT[:, t, :], LOG_MIN, None, ALU.max).then_inc(forget_ready, 1)
            ve.wait_ge(log_ready, 1)
            with ve.Fori(0, HEADS) as i:
                n.enter("cumulate", i)
                for half in range(2):
                    part = bT[:, i, half * P:half * P + P]
                    ins = ve.tensor_tensor_scan(part, ones, part, 0.0, ALU.mult, ALU.add)
                ins.then_inc(cum_ready, 1)
                n.leave(HEADS)

            masks = col("level_masks", 0, len(LEVELS) * P).bitcast(I32).rearrange("p (l c) -> p l c", c=P)

            def halves(x, m):
                return x.rearrange("p (b u m) -> p b u m", u=2, m=m)

            def level(i, h, x):
                l, m = x % 7, LEVELS[x % 7]
                ve.wait_ge(decay_ready, n.next(decay_ready))
                e = halves(el[:, x % 2, :], m)
                ve.tensor_tensor(halves(kl[:, l, :], m)[:, :, 0, :], halves(kh[:, i * 2 + h, :], m)[:, :, 0, :],
                                 e[:, :, 0, :], ALU.mult)
                ve.tensor_tensor(ql[:, l, :].rearrange("p (b m) -> p b m", m=m), halves(qh[:, h, :], m)[:, :, 1, :],
                                 e[:, :, 1, :], ALU.mult).then_inc(level_ready, 1)

            def cross_level(i, h):
                ve.wait_ge(decay_ready, n.next(decay_ready))
                ve.tensor_tensor(kx, kh[:, i * 2 + h, 0:P], cross_e[:, 0, :], ALU.mult)
                ve.tensor_tensor(qx, qh[:, h, P:SEQ], cross_e[:, 1, :], ALU.mult).then_inc(level_ready, 1)

            diag = amat[:, 0:2, :].rearrange("p a b -> p (a b)")

            def place(l, bank, at, sem_):
                m = LEVELS[l]
                ve.sem_inc(place_waited, 1)
                ins = ve.copy_predicated(halves(diag, m)[:, :, 1, :], masks[:, l, :].rearrange("p (b m) -> p b m", m=m),
                                         ps[:, bank, at:at + P].rearrange("p (b m) -> p b m", m=m))
                ins.then_inc(sem_, 1)
                ve.wait_ge(sem_, n.next(sem_))

            def gather0():
                hold(ve, bank_full[3], n.now(bank_full[3]))
                ve.wait_ge(bank_full[7], n.next(bank_full[7]))
                step(ve.tensor_tensor(amat[:, 0:2, :], ps[:, 7, 0:SEQ].rearrange("p (a b) -> p a b", b=P),
                                      ident.rearrange("p (o b) -> p o b", o=1).to_broadcast([P, 2, P]), ALU.mult))
                place(0, 7, 256, dve_step)
                place(1, 7, 384, bank_read[7])

            def gather1():
                ve.wait_ge(bank_full[3], n.next(bank_full[3]))
                for l in range(2, 6):
                    place(l, 3, (l - 2) * P, bank_read[3] if l == 5 else dve_step)

            def gather2():
                ve.wait_ge(bank_full[7], n.next(bank_full[7]))
                place(6, 7, 0, dve_step)
                ve.tensor_copy(amat[:, 2, :], ps[:, 7, P:2 * P]).then_inc(bank_read[7], 1)
                n.before(bank_read[7])
                n.before(bank_full[3])

            def rope2(x, bank):
                ve.wait_ge(bank_full[bank], n.next(bank_full[bank]))
                wide = lambda y: y.rearrange("p (o t) -> p o t", o=1).to_broadcast([P, 2, SEQ])
                step(ve.tensor_tensor(rope_t, ps[:, bank, :].rearrange("p (a t) -> p a t", t=SEQ), wide(sin), ALU.mult))
                step(ve.tensor_tensor(x, x, wide(cos), ALU.mult))
                ve.tensor_tensor(x, x, rope_t, ALU.add).then_inc(bank_read[bank], 1)

            def maxima2(j):
                ve.wait_ge(bank_full[4], n.next(bank_full[4]))
                blocks = ps[:, 4, 0:4 * P].rearrange("p (a b) -> p a b", b=P)[:, 0:3:2, :]
                step(ve.tensor_tensor(blocks, blocks, col("causal", 0, P).rearrange("p (o b) -> p o b", o=1).to_broadcast([P, 2, P]),
                                      ALU.add))
                ve.tensor_reduce(nmax[:, 0:1], ps[:, 4, 0:P], AX, ALU.max, negate=True).then_inc(max_ready, 1)
                ve.tensor_reduce(nmax[:, 1:2], ps[:, 4, P:3 * P], AX, ALU.max, negate=True).then_inc(max_ready, 1)

            def normalise2():
                ve.wait_ge(bank_read[4], n.next(bank_read[4]))
                step(ve.reciprocal(rden, rsum))
                ve.tensor_scalar(p2[:, 0:P], p2[:, 0:P], rden[:, 0:1], None, ALU.mult)
                ve.tensor_scalar(p2[:, P:3 * P], p2[:, P:3 * P], rden[:, 1:2], None, ALU.mult).then_inc(probs_ready, 1)

            def silu2(i, t, x, tanh, out):
                b = STREAM.bank("heads2", t)
                ve.wait_ge(tanh_ready, n.next(tanh_ready))
                ve.scalar_tensor_tensor(out, tanh, 1.0, ps[:, b, 0:SEQ], ALU.add, ALU.mult).then_inc(tile_read[b], 1)

            n.next(bank_full[4], 3)
            n.next(bank_full[7], 4 * 4 + 3)
            n.next(bank_read[4], 2)
            n.next(bank_read[7], 4 * 4 + 3)
            ve.wait_ge(rope_ready, 2)
            with ve.Fori(0, 4) as i:
                n.enter("heads2", i)
                hold(ve, bank_full[7], n.now(bank_full[7]))
                silu2(i, 0, 0, tanh_q[:, 0, :], qh[:, 0, :])
                silu2(i, 1, 0, tanh_q[:, 1, :], qh[:, 1, :])
                ve.wait_ge(tile_read[1], STREAM.before("heads2", i, 1) + 1)
                for x in range(4):
                    level(i, 0, x)
                rope2(q_r, 2)
                gather0()
                level(i, 0, 4)
                level(i, 0, 5)
                rope2(k_r, 2)
                level(i, 0, 6)
                cross_level(i, 0)
                gather1()
                maxima2(0)
                gather2()
                normalise2()
                level(i, 1, 7)
                level(i, 1, 8)
                maxima2(1)
                normalise2()
                gather0()
                for x in range(9, 13):
                    level(i, 1, x)
                maxima2(2)
                normalise2()
                maxima2(3)
                gather1()
                level(i, 1, 13)
                cross_level(i, 1)
                normalise2()
                gather2()
                silu2(i, 14, 0, tanh_o[:, 0, :], og[:, i * 2, :])
                silu2(i, 15, 0, tanh_o[:, 1, :], og[:, i * 2 + 1, :])
                n.leave(4)
            def gate_a(ts):
                for t in ts:
                    b = STREAM.bank("branch_a", t)
                    ve.wait_ge(tile_done, STREAM.done("branch_a", 0, t))
                    ve.scalar_tensor_tensor(xT[:, t, 0:SEQ], gates[:, t, 0:SEQ], 1.0, ps[:, b, 0:SEQ], ALU.add, ALU.mult)\
                      .then_inc(tile_read[b], 1)

            gate_a(range(4))
            for g in range(2):
                if g == 1:
                    gate_a(range(4, 8))
                ve.wait_ge(bank_read[7], n.next(bank_read[7]))
                step(ve.reciprocal(head_root[:, g, :], head_root[:, g, :]))
                for j in range(4):
                    h = 4 * g + j
                    step(ve.scalar_tensor_tensor(oh[:, h, :], oh[:, h, :], hgrn_g[:, h:h + 1],
                                                 head_root[:, g, j * SEQ:(j + 1) * SEQ], ALU.mult, ALU.mult))
                    ve.tensor_tensor(oh[:, h, :], oh[:, h, :], og[:, h, :], ALU.mult).then_inc(hgrn_ready, 1)
            for t in range(KB):
                b = STREAM.bank("branch_b", t)
                ve.wait_ge(tile_done, STREAM.done("branch_b", 0, t))
                ve.scalar_tensor_tensor(branch_t[:, t % 2, :], gates[:, KB + t, 0:SEQ], 1.0, ps[:, b, 0:SEQ], ALU.add, ALU.mult)\
                  .then_inc(tile_read[b], 1)
                ve.wait_ge(tile_read[b], STREAM.before("branch_b", 0, t) + 1)
                ve.tensor_tensor(xT[:, t, 0:SEQ], xT[:, t, 0:SEQ], branch_t[:, t % 2, :], ALU.add).then_inc(mixed, 1)
            add_tiles("mix_out2", lambda t: res2[:, t, :], SEQ)
            norm(SEQ, lambda k: res2[:, k, :], lambda k: xT[:, k, 0:SEQ], "norm_x_g_2", 6)
            n.next(bank_full[4], 3)
            n.next(bank_read[4], 2)

            for h in range(4):
                ve.wait_ge(bank_full[4], n.next(bank_full[4]))
                ve.tensor_reduce(nmax, ps[:, 4, :].rearrange("p (b m) -> p b m", m=SEQ), AX, ALU.max, negate=True)\
                  .then_inc(max_ready, 1)
                ve.wait_ge(bank_read[4], n.next(bank_read[4]))
                step(ve.reciprocal(rden, rsum))
                ve.tensor_scalar(pX[:, 0, :], pX[:, 0, :], rden[:, 0:1], None, ALU.mult)
                ve.tensor_scalar(pX[:, 1, :], pX[:, 1, :], rden[:, 1:2], None, ALU.mult).then_inc(probs_ready, 1)
            add_tiles("cross_out", lambda t: res2[:, t, :], SEQ)
            norm(SEQ, lambda k: res2[:, k, :], lambda k: xT[:, k, 0:SEQ], "norm_ffn_g_2", 7)

            def group2(phase, i, j, g):
                for x in range(2):
                    t = 4 * (g % 2) * (phase == "up2") + x
                    b, bg = STREAM.bank(phase, t + 2), STREAM.bank(phase, t)
                    ve.wait_ge(tile_read[bg], STREAM.before(phase, i, t) + 1)
                    ve.wait_ge(tile_done, STREAM.done(phase, i, t + 2))
                    ve.tensor_tensor(act[:, j + x, :], silu_g[:, 2 * (g % 2) + x, :], ps[:, b, 0:SEQ], ALU.mult)\
                      .then_inc(tile_read[b], 1)

            with ve.Fori(0, 5) as i:
                n.enter("up2", i)
                group2("up2", i, i * 4, 0)
                group2("up2", i, i * 4 + 2, 1)
                n.leave(5)
            group2("up2_end", 0, 20, 0)
            add_down("down2", lambda b: res2[:, 2 * b:2 * b + 2, :])
            norm(SEQ, lambda k: res2[:, k, :], lambda k: xT[:, k, 0:SEQ], "final_norm_g_2", 8)


        @block.gpsimd
        def _(gp):
            n = Tally("gpsimd")
            gp.wait_ge(cum_ready, HEADS)
            gp.memset(kl, 0.0).then_inc(pool_step, 1)
            gp.wait_ge(pool_step, n.next(pool_step))
            with gp.Fori(0, 4) as i:
                n.enter("heads2", i)
                for x in range(14):
                    m = LEVELS[x % 7]
                    b = bT[:, i * 2 + x // 7, :].rearrange("p (b u m) -> p b u m", u=2, m=m)
                    d = dl[:, x % 2, :].rearrange("p (b u m) -> p b u m", u=2, m=m)
                    middle = b[:, :, 0, m - 1:m].to_broadcast([P, P // m, m])
                    hold(gp, decay_ready, n.now(decay_ready) - (x != 0))
                    n.before(decay_ready, 1 + (x % 7 == 6))
                    gp.sem_inc(diff_waited, 1)
                    gp.tensor_tensor(d[:, :, 0, :], middle, b[:, :, 0, :], ALU.subtract)
                    gp.tensor_tensor(d[:, :, 1, :], b[:, :, 1, :], middle, ALU.subtract).then_inc(diff_ready, 1)
                n.leave(4)


def tabled(w, tiles):
    return w.reshape(tiles, P).T


def chunks_of(w, columns):
    k, m = w.shape
    v = w.reshape(k // P, P, m)
    return [v[:, :, c:c + CW].transpose(1, 0, 2).reshape(P, -1) for c in columns]


def kernel(**inputs):
    import numpy as np
    import concourse.bacc as bacc
    from concourse.bass_utils import run_bass_kernel_spmd

    x = {name: np.asarray(value) for name, value in inputs.items()}

    every = list(range(0, D, CW))
    w1, w2 = x["w_in"][0], x["w_in_2"][0]
    stream = []
    for i in range(4):
        stream += chunks_of(w1, [s * D + i * CW for s in (0, 1, 2, 4, 3)])
    stream += chunks_of(w1, [5 * D + c for c in every + [D + c for c in every]])
    stream += chunks_of(x["wkv_x_2"][0], every + [D + c for c in every])
    stream += chunks_of(x["w_conv_out"][0], every) + chunks_of(x["w_out"][0], every)

    def ffn(up, down):
        for j in range(0, FF, CW):
            stream.extend(chunks_of(up, [j, FF + j]))
        v = down.reshape(FT // 2, 2, P, D)
        stream.extend(v[c].transpose(1, 0, 2).reshape(P, -1) for c in range(FT // 2))

    ffn(x["w_up"][0], x["w_down"][0])
    stream += chunks_of(w2, [4 * D + c for c in every])
    for i in range(4):
        stream += chunks_of(w2, [s * D + i * CW for s in (3, 5, 0, 1, 2, 7, 8, 6)])
    for name in ("w_br_attn_2", "w_br_hgrn_2", "w_out_2", "wq_x_2", "wo_x_2"):
        stream += chunks_of(x[name][0], every)
    ffn(x["w_ffn_in_2"][0], x["w_ffn_out_2"][0])
    weights = np.stack(stream)

    t = np.zeros((P, TABLE_W), np.float32)

    def put(name, value):
        t[:, AT[name]:AT[name] + WIDTH[name]] = value

    for name in ("norm_mix_w", "conv_dw_b", "conv_ln_w", "conv_ln_b", "norm_ffn_w", "norm_final_w", "norm_mix_g_2",
                 "hgrn_norm_g_2", "norm_x_g_2", "norm_mem_g_2", "norm_ffn_g_2", "final_norm_g_2"):
        put(name, tabled(x[name].reshape(-1), KB))
    put("subln_w", x["subln_w"].reshape(P, 1))
    put("conv_dw_w", x["conv_dw_w"][0].reshape(TAPS, KB, P).transpose(2, 1, 0).reshape(P, -1))
    put("ffn_dw_w", x["ffn_dw_w"][0].reshape(3, 2 * FT, P).transpose(2, 1, 0).reshape(P, -1))
    put("ffn_dw_b", tabled(x["ffn_dw_b"].reshape(-1), 2 * FT))
    put("lb_logits", x["hgrn_lb_logits_2"].reshape(2, KB, P).transpose(2, 0, 1).reshape(P, -1))
    lambdas = np.concatenate([x[name].reshape(-1) for name in ("lambda_q1", "lambda_k1", "lambda_q2", "lambda_k2")])
    put("lambdas", np.broadcast_to(lambdas, (P, 4 * HD)))

    p, q = np.arange(P)[:, None], np.arange(P)[None, :]
    put("ones", 1.0)
    put("ident", p == q)
    put("rotate", np.where(p == q + HD // 2, -1.0, 0.0) * (q % HD < HD // 2) + np.where(p == q - HD // 2, 1.0, 0.0) * (q % HD >= HD // 2))
    put("inv_freq", 10000.0 ** (-2.0 * (p % (HD // 2)) / HD))
    put("eps6", 1e-6)
    put("eps5", 1e-5)
    put("causal", np.where(q <= p, 0.0, NEG))
    masks = []
    for m in LEVELS:
        column = np.arange(P // 2)[None, :] // m
        one = ((p // (2 * m) == column) & (p % (2 * m) < m)).astype(np.float32)
        masks += [one, one]
    put("level_masks", np.concatenate(masks, 1))

    h = np.concatenate([x["meta_tokens"], x["x"][0]], 0)
    arrays = {
        "weights": weights,
        "table": t,
        "h_in": np.ascontiguousarray(h.T.reshape(KB, P, T1).transpose(1, 0, 2)),
        "mem": np.ascontiguousarray(x["mem_2"][0].T.reshape(KB, P, SEQ).transpose(1, 0, 2)),
        "positions": np.ascontiguousarray(np.broadcast_to(x["positions_2"].astype(np.int32), (P, SEQ))),
    }
    nc = bacc.Bacc("TRN2", target_bir_lowering=False, num_devices=1)
    aps = {}
    for name, value in arrays.items():
        dt = mybir.dt.from_np(value.dtype)
        aps[name] = nc.dram_tensor(name, value.shape, dt, kind="ExternalInput").ap()
    aps["out"] = nc.dram_tensor("out", (P, KB, SEQ), F32, kind="ExternalOutput").ap()
    blocks_kernel(nc, aps)
    r = run_bass_kernel_spmd(nc, [arrays], core_ids=[0])
    y = np.asarray(r.results[0]["out"])
    return y.transpose(1, 0, 2).reshape(D, SEQ).T[None]
```

```python
from contextlib import ExitStack

import concourse.bass as bass
from concourse import mybir

F32 = mybir.dt.float32
F32R = mybir.dt.float32r
I32 = mybir.dt.int32
ALU = mybir.AluOpType
ACT = mybir.ActivationFunctionType
AX = mybir.AxisListType.X

P = 128
D = 1024
KB = D // P
SEQ = 256
META = 16
T1 = META + SEQ
LEAD = 2
Q0 = META - LEAD
TQ = T1 - Q0
HEADS = 8
HD = 64
CHUNK = 64
TAPS = 31
FF = 2816
FT = FF // P
NEG = -1e30
LAMBDA_INIT = 0.8 - 0.6
MAGIC = 1.5 * 2.0 ** 23
TWO_PI = (6.28125, 0.0019350051879882812, 3.0199159819e-07)
PI_IN = 3.1415925
LEVELS = (64, 32, 16, 8, 4, 2, 1)
RING = 8
KEY_SCALE = 0.5 * P ** -0.5
LOG_MIN = 2.0 ** -63
NORMS = {"mix1": 0, "mem": 1, "ffn1": 2, "final1": 3, "mix2": 4, "cross": 5, "ffn2": 6, "out": 7}
CW = 2 * P

TABLE = [
    ("norm_mix_w", KB), ("subln_w", 1), ("conv_dw_w", KB * TAPS), ("conv_dw_b", KB), ("conv_ln_w", KB),
    ("conv_ln_b", KB), ("norm_ffn_w", KB), ("ffn_dw_w", 2 * FT * 3), ("ffn_dw_b", 2 * FT), ("norm_final_w", KB),
    ("norm_mix_g_2", KB), ("lb_logits", 2 * KB), ("hgrn_norm_g_2", KB), ("norm_x_g_2", KB), ("norm_mem_g_2", KB),
    ("norm_ffn_g_2", KB), ("final_norm_g_2", KB), ("lambdas", 4 * HD), ("ones", P), ("ident", P), ("rotate", P),
    ("inv_freq", 1), ("eps6", 1), ("eps5", 1), ("causal", P), ("level_masks", len(LEVELS) * P),
]
WIDTH = dict(TABLE)
AT = {}
TABLE_W = 0
for _name, _w in TABLE:
    AT[_name] = TABLE_W
    TABLE_W += _w

PHASES = [
    ("heads1", 4, (0, 1, 2, 3, 0, 1, 2, 3), (2,) * 8),
    ("mem_v", 1, (0, 1, 2, 3), (2,) * 4),
    ("conv_out", 1, (0, 1, 2, 3), (2,) * 4),
    ("mix_out1", 1, (6, 5, 7, 0), (2,) * 4),
    ("up1", 5, (1, 2, 3, 0), (2,) * 4),
    ("up1_end", 1, (1, 2), (2,) * 2),
    ("down1", 2, (3, 0, 1, 2), (1,) * 4),
    ("down1_end", 1, (3, 0, 1), (1, 1, 4)),
    ("forget", 1, (2, 3, 0, 1), (2,) * 4),
    ("heads2", 4, (4, 5, 6, 7, 2, 3, 0, 1), (2,) * 8),
    ("branch_a", 1, (4, 5, 6, 7), (2,) * 4),
    ("branch_b", 1, (2, 3, 0, 1), (2,) * 4),
    ("mix_out2", 1, (4, 5, 6, 7), (2,) * 4),
    ("cross_q", 1, (3, 0, 1, 2), (2,) * 4),
    ("cross_out", 1, (5, 4, 6, 2), (2,) * 4),
    ("up2", 5, (3, 0, 1, 2), (2,) * 4),
    ("up2_end", 1, (3, 0), (2,) * 2),
    ("down2", 2, (1, 2, 3, 0), (1,) * 4),
    ("down2_end", 1, (1, 2, 3), (1, 1, 4)),
]
SPLIT = ("heads1", "mem_v", "up1", "up1_end", "down1", "down1_end", "up2", "up2_end", "down2", "down2_end")
HIGH, LOW = 4, 6
HALF_CHUNK = KB * P
TWO_BANKS = ("heads2",)


class Stream:

    def __init__(self):
        self.at, self.split_at, split = {}, {}, 0
        chunk, done, landed, used = 0, 0, [0] * RING, [0] * 4
        for name, iters, slots, tiles in PHASES:
            banks = []
            if not name.startswith("down"):
                banks = [t % (2 if name in TWO_BANKS else 4) for t in range(sum(tiles))]
            elif name.endswith("end"):
                banks = [0, 1, 2, 3]
            self.at[name] = (chunk, done, tuple(landed), tuple(used), iters, slots, tiles, banks)
            self.split_at[name] = split
            split += iters * len(slots) * (name in SPLIT)
            chunk += iters * len(slots)
            done += iters * sum(tiles)
            for s in slots:
                landed[s] += iters
            for b in banks:
                used[b] += iters
        self.chunks = chunk

    def landed(self, phase, i, c):
        _, _, landed, _, _, slots, _, _ = self.at[phase]
        slot, body = slots[c % len(slots)], c // len(slots)
        times = slots.count(slot)
        return (i * times + (landed[slot] + 1 + slots[:c % len(slots)].count(slot) + body * times)) * 16

    def split(self, phase, i, c):
        return i * len(self.at[phase][5]) + (self.split_at[phase] + c + 1)

    def parity(self, phase, c):
        return (self.split_at[phase] + c) % 2

    def done(self, phase, i, t):
        _, done, _, _, _, _, tiles, _ = self.at[phase]
        return i * sum(tiles) + (done + t + 1)

    def bank(self, phase, t):
        return self.at[phase][7][t]

    def before(self, phase, i, t):
        _, _, _, used, _, _, _, banks = self.at[phase]
        b = banks[t]
        return i * banks.count(b) + (1 + used[b] + banks[:t].count(b))


STREAM = Stream()

CREDITED = ("tile_read", "bank_full", "bank_read", "probs_ready", "level_ready", "decay_ready", "conv_ready", "act_ready")
INPUTS = {"mix1": 0, "mem": 1, "ffn1": 2, "ffn2": 3}


def credit(name):
    return 1 if name.startswith(CREDITED) else 0


BODY = {}
BODY[('tensor', 'heads1')] = {'kv_ready': 1, 'bank_read4': 4, 'probs_ready': 4, 'bank_read6': 4, 'bank_read7': 4}
BODY[('tensor', 'heads2')] = {'bank_read7': 4, 'khs_ready': 2, 'level_ready': 16, 'bank_read2': 2, 'bank_read3': 4, 'bank_read4': 4, 'probs_ready': 4, 'bank_read5': 4, 'bank_read6': 2}
BODY[('scalar', 'heads1')] = {'bank_full4': 4, 'max_ready': 4, 'probs_ready': 4, 'bank_full6': 4, 'bank_full7': 4}
BODY[('scalar', 'up1')] = {'act_ready0': 2, 'tap0': 8, 'gate_act': 4, 'act_ready1': 2}
BODY[('scalar', 'heads2')] = {'bank_full7': 4, 'diff_ready': 14, 'level_ready': 16, 'bank_full4': 4, 'max_ready': 8, 'bank_full3': 4, 'bank_full5': 4, 'bank_full6': 4}
BODY[('vector', 'heads1')] = {'bank_full4': 4, 'dve_step': 78, 'bank_read4': 4, 'bank_full6': 4, 'conv_ready': 2}
BODY[('vector', 'up1')] = {'tap0': 8, 'dve_step': 8, 'gate_act': 4}
BODY[('vector', 'cumulate')] = {}
BODY[('vector', 'heads2')] = {'tanh_ready': 4, 'decay_ready': 16, 'bank_full2': 2, 'dve_step': 24, 'bank_full7': 4, 'bank_read7': 4, 'bank_full3': 4, 'bank_read3': 2, 'bank_full4': 4, 'bank_read4': 4}
BODY[('vector', 'up2')] = {}
BODY[('gpsimd', 'up1')] = {'act_ready0': 2, 'hidden_high': 4, 'act_ready1': 2}
BODY[('gpsimd', 'heads2')] = {'decay_ready': 16}
BODY[('gpsimd', 'up2')] = {'hidden_high': 4}



class Tally:

    def __init__(self, engine):
        self.engine, self.base, self.inside, self.i, self.body = engine, {}, {}, None, {}

    def before(self, sem, k=1):
        v = self.now(sem)
        (self.base if self.i is None else self.inside)[sem.name] = \
            (self.base if self.i is None else self.inside).get(sem.name, 0 if self.i is not None else credit(sem.name)) + k
        return v

    def next(self, sem, k=1):
        self.before(sem, k)
        return self.now(sem)

    def now(self, sem):
        v = self.base.get(sem.name, credit(sem.name))
        if self.i is not None:
            v = self.i * self.body.get(sem.name, 0) + (v + self.inside.get(sem.name, 0))
        return v

    def enter(self, loop, i):
        self.i, self.loop, self.inside = i, loop, {}
        self.body = BODY.get((self.engine, loop), {})

    def leave(self, iters):
        check_body(self.engine, self.loop, self.inside, self.body)
        for name, k in self.inside.items():
            self.base[name] = self.base.get(name, credit(name)) + iters * k
        self.i = None


def check_body(engine, loop, found, stated):
    assert found == stated, (engine, loop, found)


def hold(eng, sem, value):
    if not (isinstance(value, int) and value <= 0):
        eng.wait_ge(sem, value)


def blocks_kernel(nc, a):
    ctx = ExitStack()
    with ctx:
        address = {}

        def sb(name, shape, dt=F32):
            address[name] = -(-nc.sbuf_base // 32) * 32
            return ctx.enter_context(nc.sbuf_tensor(name, shape, dt))

        def rounded(name, shape, over, skip=0):
            return nc.alloc_sbuf_tensor_at(name, shape, F32R, offset=address[over] + 4 * skip)

        def sem(name):
            return ctx.enter_context(nc.semaphore(name))

        ring = sb("ring", [P, RING, KB * CW])
        table = sb("table_sb", [P, TABLE_W])
        res = sb("res", [P, KB, T1])
        res2 = sb("res2", [P, KB, SEQ])
        xT = sb("xT", [P, KB, T1])
        sq = sb("sq", [P, KB, T1])
        k_mem = sb("k_mem", [P, KB, SEQ])
        v_mem = sb("v_mem", [P, 2, D])
        glu = sb("glu", [P, KB, TAPS - 1 + T1])
        conv = sb("conv", [P, KB, TQ])
        branch = sb("branch", [P, 3 * KB, TQ])
        gates, att = branch[:, 0:2 * KB, :], branch[:, 2 * KB:3 * KB, :]
        act = sb("act", [P, FT, SEQ])
        work = sb("work", [P, 4864])
        root = sb("root", [P, T1])
        rinv = sb("rinv", [P, T1])
        small = sb("small", [P, 96])
        parts = rounded("parts", [P, RING - HIGH, KB * CW], "ring", HIGH * KB * CW)
        x_high = rounded("x_high", [P, KB, T1], "xT")
        x_low = rounded("x_low", [P, KB, TQ], "glu")
        act_high = rounded("act_high", [P, FT, SEQ], "act")
        act_low = rounded("act_low", [P, FT, TQ], "branch")
        x_low1 = rounded("x_low1", [P, KB, T1], "act", KB * SEQ)
        mem_high = rounded("mem_high", [P, KB, SEQ], "act")
        mem_low = rounded("mem_low", [P, KB, SEQ], "res2")
        ps = ctx.enter_context(nc.psum_tensor("ps", [P, 8, 512], F32))

        def carve(region, at, *shape):
            n = 1
            for d in shape:
                n *= d
            flat = region[:, at:at + n]
            if len(shape) == 1:
                return flat
            if len(shape) == 2:
                return flat.rearrange("p (a b) -> p a b", b=shape[1])
            return flat.rearrange("p (a b c) -> p a b c", b=shape[1], c=shape[2])

        def col(name, j=0, n=1):
            return table[:, AT[name] + j:AT[name] + j + n] if isinstance(j, int) else \
                table[:, bass.ds(j + AT[name], n)]

        ones, ident = col("ones", 0, P), col("ident", 0, P)

        qT = carve(work, 0, 2, TQ)
        kT = carve(work, 516, 2, T1)
        vN = carve(work, 1060, 2, CW)
        v_meta = carve(work, 1572, CW)
        tanh_b = carve(work, 2596, 2, T1)
        E1 = carve(work, 3140, 2, T1)
        a1 = carve(work, 3684, T1)
        a1T = carve(work, 3956, 2 * P)
        a1M = carve(work, 4212, P)
        conv_odd = carve(work, 4340, TQ)
        qM = carve(work, 4598, HEADS, LEAD)
        kM = carve(work, 4614, HEADS, META)
        sM = carve(work, 0, 2 * HEADS, META)
        aM = carve(work, 256, HEADS, META)
        aMT = carve(work, 384, HEADS, LEAD)
        taps = carve(work, 0, 8, SEQ)
        silu_g = carve(work, 2048, 4, SEQ)
        actf = act[:, :, :].rearrange("p a b -> p (a b)")
        mem = carve(actf, 0, KB, SEQ)
        att_root = carve(actf, 2048, 2, 4 * TQ)
        vM = carve(actf, 4608, D)
        bT = conv_f = conv[:, :, :].rearrange("p a b -> p (a b)")
        bT = carve(conv_f, 0, HEADS, SEQ)
        gluf = glu[:, :, :].rearrange("p a b -> p (a b)")
        kh = carve(gluf, 0, HEADS, SEQ)
        attf = branch[:, :, :].rearrange("p a b -> p (a b)")[:, 2 * KB * TQ:3 * KB * TQ]
        ya = carve(attf, 0, KB, SEQ)
        og = carve(actf, 0, KB, SEQ)
        oh = carve(actf, 2048, KB, SEQ)
        resf = res[:, :, :].rearrange("p a b -> p (a b)")
        sqf = sq[:, :, :].rearrange("p a b -> p (a b)")
        q_r = carve(work, 0, 2, SEQ)
        k_r = carve(work, 512, 2, SEQ)
        rope_t = carve(work, 1024, 2, SEQ)
        vA = carve(work, 1536, 2, CW)
        iN = carve(work, 2048, 2, CW)
        p2 = carve(work, 2560, 3 * P)
        p2T = carve(work, 2944, 3 * P)
        tanh_q = carve(work, 3328, 2, SEQ)
        qh = carve(work, 3840, 2, SEQ)
        kh_s = carve(actf, 4480, 2, SEQ)
        kl = carve(resf, 0, len(LEVELS), SEQ)
        cross_e = carve(resf, 1792, 2, P)
        qx = carve(resf, 2048, P)
        dl = carve(sqf, 0, 2, SEQ)
        el = carve(sqf, 512, 2, SEQ)
        ql = carve(sqf, 1024, len(LEVELS), P)
        kx = carve(sqf, 1920, P)
        amat = carve(actf, 4096, 3, P)
        cos = carve(work, 4352, SEQ)
        sin = carve(work, 4608, SEQ)
        tanh_o = carve(actf, 4992, 2, SEQ)
        branch_t = carve(work, 0, 2, SEQ)
        head_root = carve(work, 512, 2, 4 * SEQ)
        rope_a, rope_b, rope_c = (carve(work, 3072 + SEQ * j, SEQ) for j in range(3))
        pos_i = rope_c.bitcast(I32)
        qX = carve(conv_f, 0, KB, SEQ)
        oX = carve(attf, 0, KB, SEQ)
        pX = carve(work, 0, 2, SEQ)
        pXT = carve(work, 512, 2, SEQ)
        nmax, rsum, rden, coef = (small[:, 2 * j:2 * j + 2] for j in range(4))
        neg_lam, lam_t, sub_w = small[:, 8:9], small[:, 10:14], small[:, 14:15]
        m_max, m_sum = small[0:LEAD, 16:32], small[0:LEAD, 32:48]
        lb, one_lb, lb_t = small[:, 48:56], small[:, 56:64], small[:, 64:88]
        hgrn_g = small[:, 88:96]

        table_in, res_in, mem_in, pos_in, out_sent = (sem(n) for n in ("table_in", "res_in", "mem_in", "pos_in", "out_sent"))
        landed = [sem(f"chunk_landed{s}") for s in range(RING)]
        tile_done = sem("tile_done")
        tile_read = [sem(f"tile_read{b}") for b in range(4)]
        bank_full = {b: sem(f"bank_full{b}") for b in range(2, 8)}
        bank_read = {b: sem(f"bank_read{b}") for b in range(2, 8)}
        dve_step, act_step, pool_step = sem("dve_step"), sem("act_step"), sem("pool_step")
        consts_ready = sem("consts_ready")
        squared, rooted, normed = sem("squared"), sem("rooted"), sem("normed")
        max_ready, probs_ready = sem("max_ready"), sem("probs_ready")
        kv_ready = sem("kv_ready")
        conv_ready = sem("conv_ready")
        meta_shift, meta_exp, meta_probs, meta_T, meta_done = (sem(n) for n in ("meta_shift", "meta_exp", "meta_probs", "meta_T", "meta_done"))
        att_gated = sem("att_gated")
        centered, conv_root, conv_scaled, conv_act = (sem(n) for n in ("centered", "conv_root", "conv_scaled", "conv_act"))
        mixed = sem("mixed")
        tap0, gate_act = sem("tap0"), sem("gate_act")
        act_ready = [sem("act_ready0"), sem("act_ready1")]
        forget_ready, log_ready, cum_ready, lb_exp = sem("forget_ready"), sem("log_ready"), sem("cum_ready"), sem("lb_exp")
        angle_ready, rope_ready = sem("angle_ready"), sem("rope_ready")
        diff_ready, decay_ready, level_ready, khs_ready = (sem(n) for n in ("diff_ready", "decay_ready", "level_ready", "khs_ready"))
        hgrn_ready, tanh_ready = sem("hgrn_ready"), sem("tanh_ready")
        split_high, split_low = sem("split_high"), [sem("split_low0"), sem("split_low1")]
        x_high_ready, x_low_ready, hidden_high, hidden_low = (sem(n) for n in ("x_high_ready", "x_low_ready", "hidden_high", "hidden_low"))
        place_waited, diff_waited = sem("place_waited"), sem("diff_waited")

        def spread(x, width):
            return x.rearrange("p (j o) -> p j o", o=1).to_broadcast([x.shape[0], x.shape[1], width])

        def low_half(eng, phase, i, c, half):
            slot, p = STREAM.at[phase][5][c % len(STREAM.at[phase][5])], STREAM.parity(phase, c)
            cols = slice(half * HALF_CHUNK, (half + 1) * HALF_CHUNK)
            eng.wait_ge(split_high, STREAM.split(phase, i, c) * 2 - half)
            eng.tensor_tensor(parts[:, LOW - HIGH + p, cols], ring[:, slot, cols], parts[:, p, cols].bitcast(F32), ALU.subtract)\
               .then_inc(split_low[half], 1)

        block = ctx.enter_context(nc.Block())

        @block.sync
        def _(sp):
            for k in range(0, KB, 2):
                sp.dma_start(res[:, k:k + 2, :], a["h_in"][:, k:k + 2, :]).then_inc(res_in, 16)
            for s in [*tile_read, *bank_full.values(), *bank_read.values(), probs_ready, level_ready, decay_ready, conv_ready, *act_ready]:
                sp.sem_inc(s, 1)
            last = [[] for _ in range(RING)]

            def load(phase, i, c, free):
                first, _, _, _, _, slots, _, _ = STREAM.at[phase]
                for sem_, value in free:
                    sp.wait_ge(sem_, value)
                sp.dma_start(ring[:, slots[c], :], a["weights"][i * len(slots) + (first + c)]).then_inc(landed[slots[c]], 16)

            def used(phase, i, c):
                if phase in SPLIT:
                    return [(split_low[0], STREAM.split(phase, i, c)), (split_low[1], STREAM.split(phase, i, c))]
                return [(tile_done, STREAM.done(phase, i, sum(STREAM.at[phase][6][:c + 1]) - 1))]

            for phase, iters, slots, tiles in PHASES:
                for c in range(len(slots)):
                    load(phase, 0, c, last[slots[c]])
                    last[slots[c]] = used(phase, 0, c)
                if iters > 1:
                    with sp.Fori(1, iters) as i:
                        for c in range(len(slots)):
                            earlier = [e for e in range(c) if slots[e] == slots[c]]
                            later = [e for e in range(len(slots)) if slots[e] == slots[c]]
                            load(phase, i, c, used(phase, i, earlier[-1]) if earlier else used(phase, i - 1, later[-1]))
                for c in range(len(slots)):
                    last[slots[c]] = used(phase, iters - 1, c)
                    if phase in SPLIT:
                        done = STREAM.done(phase, iters - 1, sum(tiles[:c + 1]) - 1)
                        last[HIGH + STREAM.parity(phase, c)] = last[LOW + STREAM.parity(phase, c)] = [(tile_done, done)]
            sp.wait_ge(normed, NORMS["out"] * KB + KB)
            sp.dma_start(a["out"], xT[:, :, 0:SEQ]).then_inc(out_sent, 16)
            sp.wait_ge(out_sent, 16)

        @block.tensor
        def _(pe):
            n = Tally("tensor")

            def tile(phase, i, t, moving, width, ready=None):
                b, c, e = STREAM.bank(phase, t), t // 2, t % 2
                slot = STREAM.at[phase][5][c]
                hold(pe, tile_read[b], STREAM.before(phase, i, t))
                if e == 0:
                    pe.wait_ge(landed[slot], STREAM.landed(phase, i, c))
                for k in range(KB):
                    if ready is not None and t == 0:
                        pe.wait_ge(ready[0], ready[1] + k)
                    mm = pe.matmul(ps[:, b, 0:width], ring[:, slot, k * CW + e * P:k * CW + e * P + P], moving(k),
                                   start=k == 0, stop=k == KB - 1)
                mm.then_inc(tile_done, 1)

            def by_token(phase, i, t, first, src, extra=None):
                b, c = STREAM.bank(phase, t), t // 2
                slot = STREAM.at[phase][5][c]
                hold(pe, tile_read[b], STREAM.before(phase, i, t))
                if t % 2 == 0:
                    pe.wait_ge(landed[slot], STREAM.landed(phase, i, c))
                if extra:
                    for k in range(KB):
                        pe.matmul(ps[0:extra, b, CW:2 * CW], src(k, 0, extra), ring[:, slot, k * CW:(k + 1) * CW],
                                  start=k == 0, stop=k == KB - 1)
                for k in range(KB):
                    mm = pe.matmul(ps[:, b, 0:CW], src(k, first, P), ring[:, slot, k * CW:(k + 1) * CW],
                                   start=k == 0, stop=k == KB - 1)
                mm.then_inc(tile_done, 1)

            def channel_sum(bank, src, width, ready, order=tuple(range(KB))):
                hold(pe, bank_read[bank], n.now(bank_read[bank]))
                for k in order:
                    pe.wait_ge(ready, n.next(ready))
                    mm = pe.matmul(ps[:, bank, 0:width], ones, src[:, k, 0:width], start=k == order[0], stop=k == order[-1])
                mm.then_inc(bank_full[bank], 1)

            def norm_sum(width, src=sq):
                hold(pe, rooted, n.before(rooted))
                channel_sum(4, src, width, squared)

            def weight_parts(phase, c):
                p = STREAM.parity(phase, c)
                return parts[:, p, :], parts[:, LOW - HIGH + p, :]

            def wait_low(phase, i, c):
                pe.wait_ge(split_low[0], STREAM.split(phase, i, c))
                pe.wait_ge(split_low[1], STREAM.split(phase, i, c))

            def split_products(phase, c, out, operands):
                i, low_wait = operands[0], operands[1]
                for step_, (left, right) in enumerate(operands[2]):
                    if step_ == 2 and low_wait:
                        wait_low(phase, i, c)
                    for k in range(KB):
                        mm = pe.matmul(out, left(k), right(k), start=step_ == 0 and k == 0, stop=step_ == 2 and k == KB - 1)
                return mm

            def split_tile(phase, i, t, high_x, low_x, width, first_token=0):
                b, c, e = STREAM.bank(phase, t), t // 2, t % 2
                high, low = weight_parts(phase, c)
                w = lambda part: lambda k: part[:, k * CW + e * P:k * CW + e * P + P]
                x = lambda part: lambda k: part[:, k, first_token:first_token + width]
                hold(pe, tile_read[b], STREAM.before(phase, i, t))
                if e == 0:
                    pe.wait_ge(split_high, STREAM.split(phase, i, c) * 2)
                split_products(phase, c, ps[:, b, 0:width],
                               (i, e == 0, ((w(high), x(high_x)), (w(high), x(low_x)), (w(low), x(high_x)))))\
                    .then_inc(tile_done, 1)

            def split_by_token(phase, i, t, first_token, high_x, low_x, extra=False):
                b, c = STREAM.bank(phase, t), t // 2
                high, low = weight_parts(phase, c)
                w = lambda part: lambda k: part[:, k * CW:(k + 1) * CW]
                hold(pe, tile_read[b], STREAM.before(phase, i, t))
                if t % 2 == 0:
                    pe.wait_ge(split_high, STREAM.split(phase, i, c) * 2)
                for start_token, at in ([(0, CW)] if extra else []) + [(first_token, 0)]:
                    x = lambda part: lambda k: part[:, k, start_token:start_token + P]
                    mm = split_products(phase, c, ps[:, b, at:at + CW],
                                        (i, t % 2 == 0, ((x(high_x), w(high)), (x(low_x), w(high)), (x(high_x), w(low)))))
                mm.then_inc(tile_done, 1)

            def split_chunk(phase, i, c, width, first=None):
                high, low = weight_parts(phase, c)
                banks = [STREAM.bank(phase, 2 * c + e) for e in range(2)]

                def products(es, w, x, begin=False, end=False, ready=None):
                    for k in range(KB):
                        if ready:
                            pe.wait_ge(ready, first + k + 1)
                        for e in es:
                            mm = pe.matmul(ps[:, banks[e], 0:width], w[:, k * CW + e * P:k * CW + e * P + P],
                                           x[:, k, 0:width], start=begin and k == 0, stop=end and k == KB - 1)
                            if end and k == KB - 1:
                                mm.then_inc(tile_done, 1)

                if first is not None:
                    pe.wait_ge(split_high, STREAM.split(phase, i, c) * 2)
                    for e in range(2):
                        hold(pe, tile_read[banks[e]], STREAM.before(phase, i, 2 * c + e))
                    products((0, 1), high, x_high, begin=True, ready=x_high_ready)
                    wait_low(phase, i, c)
                    products((0, 1), low, x_high)
                    products((0, 1), high, x_low, end=True, ready=x_low_ready)
                    return
                for e in range(2):
                    split_tile(phase, i, 2 * c + e, x_high, x_low, width)

            pe.wait_ge(table_in, 16)
            norm_sum(T1)
            norm_sum(SEQ, k_mem)

            def scores1(u):
                h, i = u // 2, u % 2
                width = META + P * (i + 1)
                hold(pe, bank_read[4], n.before(bank_read[4]))
                for m in range(2):
                    mm = pe.matmul(ps[:, 4 + m, 0:width], qT[HD * m:HD * m + HD, h, LEAD + P * i:LEAD + P * i + P],
                                   kT[HD * m:HD * m + HD, h, 0:width], start=True, stop=True)
                mm.then_inc(bank_full[4], 1)

            def turn1(u):
                pe.wait_ge(probs_ready, n.next(probs_ready))
                hold(pe, bank_read[6], n.before(bank_read[6]))
                pe.transpose(ps[0:META, 6, 2 * P:3 * P], a1[:, 0:META], ident)
                for j in range(u % 2 + 1):
                    mm = pe.transpose(ps[:, 6, j * P:j * P + P], a1[:, META + j * P:META + j * P + P], ident)
                mm.then_inc(bank_full[6], 1)

            def values1(u):
                h = u // 2
                hold(pe, bank_read[6], n.now(bank_read[6]))
                hold(pe, bank_read[7], n.before(bank_read[7]))
                pe.matmul(ps[:, 7, 0:P], v_meta[0:META, h * P:h * P + P], a1M[0:META, :], start=True, stop=False)
                for j in range(u % 2 + 1):
                    mm = pe.matmul(ps[:, 7, 0:P], vN[:, j, h * P:h * P + P], a1T[:, j * P:j * P + P],
                                   start=False, stop=j == u % 2)
                mm.then_inc(bank_full[7], 1)

            pe.wait_ge(x_low_ready, KB)
            with pe.Fori(0, 4) as i:
                n.enter("heads1", i)

                def proj(t):
                    if t in (0, 1, 10, 11, 12, 13):
                        split_tile("heads1", i, t, x_high, x_low1, TQ, Q0)
                    elif t in (4, 5):
                        split_by_token("heads1", i, t, META + P * (t % 2), x_high, x_low1, extra=t == 5)
                    elif t < 10:
                        split_tile("heads1", i, t, x_high, x_low1, T1)
                    else:
                        pe.wait_ge(x_low_ready, 2 * KB)
                        split_tile("heads1", i, t, mem_high, mem_low, SEQ)

                for t in range(6):
                    proj(t)
                pe.wait_ge(kv_ready, n.next(kv_ready))
                scores1(0)
                for u in range(3):
                    proj(6 + 2 * u)
                    proj(7 + 2 * u)
                    if u >= 1:
                        values1(u - 1)
                    turn1(u)
                    scores1(u + 1)
                proj(12)
                proj(13)
                values1(2)
                turn1(3)
                proj(14)
                values1(3)
                proj(15)
                n.leave(4)

            for j in range(2 * HEADS):
                m, h = j // HEADS, j % HEADS
                if j == 0:
                    hold(pe, bank_read[4], n.now(bank_read[4]))
                mm = pe.matmul(ps[0:LEAD, 4 + m, h * META:(h + 1) * META], qM[HD * m:HD * m + HD, h, :],
                               kM[HD * m:HD * m + HD, h, :], start=True, stop=True)
            mm.then_inc(bank_full[4], 1)

            def mem_v(t):
                split_by_token("mem_v", 0, t, P * (t % 2), mem_high, mem_low)

            mem_v(0)
            mem_v(1)
            mem_v(2)
            pe.wait_ge(meta_probs, 1)
            hold(pe, bank_read[6], n.now(bank_read[6]))
            for h in range(HEADS):
                mm = pe.transpose(ps[0:META, 6, LEAD * h:LEAD * h + LEAD], aM[0:LEAD, h, :], ident[0:LEAD, 0:LEAD])
            mm.then_inc(bank_full[6], 1)
            mem_v(3)
            pe.wait_ge(meta_T, 1)
            hold(pe, bank_read[7], n.before(bank_read[7]))
            for h in range(HEADS):
                mm = pe.matmul(ps[:, 7, LEAD * h:LEAD * h + LEAD], vM[0:META, h * P:h * P + P], aMT[0:META, h, :],
                               start=True, stop=True)
            mm.then_inc(bank_full[7], 1)
            mem_v(4)

            def head_sums(src, width, ready):
                for b in range(4, 8):
                    hold(pe, bank_read[b], n.before(bank_read[b]))
                    pe.wait_ge(ready, n.next(ready))
                    pe.matmul(ps[:, b, 0:width], ones, src(b - 4), start=True, stop=True).then_inc(bank_full[b], 1)

            head_sums(lambda j: sq[:, j, 0:TQ], TQ, squared)
            mem_v(5)
            head_sums(lambda j: sq[:, 4 + j, 0:TQ], TQ, squared)
            channel_sum(4, conv, TQ, conv_ready)
            mem_v(6)
            mem_v(7)
            channel_sum(5, sq, TQ, squared)
            n.before(bank_read[5])
            for t in range(8):
                tile("conv_out", 0, t, lambda k: conv[:, k, :], TQ, ready=(conv_act, 1))
            for t in range(8):
                tile("mix_out1", 0, t, lambda k: xT[:, k, 0:TQ], TQ, ready=(mixed, 1))
            norm_sum(TQ)

            def ffn(up, down, width, count):
                split_chunk(up, 0, 0, width, first=INPUTS["ffn" + up[-1]] * KB)
                for c in range(1, 4):
                    split_chunk(up, 0, c, width)
                with pe.Fori(1, 5) as i:
                    for c in range(4):
                        split_chunk(up, i, c, width)
                for c in range(2):
                    split_chunk(up + "_end", 0, c, width)
                for b in range(4):
                    hold(pe, tile_read[b], STREAM.before(down + "_end", 0, b))
                pe.wait_ge(hidden_low, count * FT)

                def chunk(phase, i, c, first, last):
                    high, low = weight_parts(phase, c)
                    kb = i * 8 + 2 * c if phase == down else 16 + 2 * c
                    pe.wait_ge(split_high, STREAM.split(phase, i, c) * 2)
                    for step_, (w, x) in enumerate(((high, act_high), (high, act_low), (low, act_high))):
                        if step_ == 2:
                            wait_low(phase, i, c)
                        for kk in range(2):
                            for t in range(KB):
                                mm = pe.matmul(ps[:, t // 2, t % 2 * SEQ:(t % 2 + 1) * SEQ],
                                               w[:, kk * D + t * P:kk * D + t * P + P], x[:, kb + kk, 0:SEQ],
                                               start=first and step_ == 0 and kk == 0 and t % 2 == 0,
                                               stop=last and step_ == 2 and kk == 1, skip_group_check=True)
                                if last and step_ == 2 and kk == 1 and t % 2 == 1:
                                    mm.then_inc(tile_done, 1)
                    if not last:
                        mm.then_inc(tile_done, 1)

                for c in range(4):
                    chunk(down, 0, c, c == 0, False)
                for c in range(4):
                    chunk(down, 1, c, False, False)
                for c in range(3):
                    chunk(down + "_end", 0, c, False, c == 2)
                norm_sum(SEQ)

            ffn("up1", "down1", TQ, 1)

            norm_sum(SEQ)
            x2 = lambda k: xT[:, k, 0:SEQ]
            x2tok = lambda k, f, m: xT[:, k, f:f + m]
            for t in range(8):
                tile("forget", 0, t, x2, SEQ, ready=(normed, NORMS["mix2"] * KB + 1))

            def rotate(i, src, t):
                hold(pe, bank_read[2], n.before(bank_read[2]))
                for b in range(2):
                    pe.wait_ge(tile_read[b], STREAM.before("heads2", i, t + b) + 1)
                pe.matmul(ps[:, 2, :], col("rotate", 0, P), src[:, :, :].rearrange("p a b -> p (a b)"),
                          start=True, stop=True).then_inc(bank_full[2], 1)

            def scores2(j):
                s, half = j // 2, j % 2
                rows = slice(HD * half, HD * half + HD)
                if j == 0:
                    hold(pe, bank_read[2], n.now(bank_read[2]))
                hold(pe, bank_read[4], n.before(bank_read[4]))
                pe.matmul(ps[:, 4, 0:P], q_r[rows, s, 0:P], k_r[rows, s, 0:P], start=True, stop=True)
                pe.matmul(ps[:, 4, P:3 * P], q_r[rows, s, P:SEQ], k_r[rows, s, :], start=True, stop=True)\
                  .then_inc(bank_full[4], 1)

            def turn2(j):
                pe.wait_ge(probs_ready, n.next(probs_ready))
                hold(pe, bank_read[5], n.before(bank_read[5]))
                for b in range(3):
                    mm = pe.transpose(ps[:, 5, b * P:b * P + P], p2[:, b * P:b * P + P], ident)
                mm.then_inc(bank_full[5], 1)

            def values2(j):
                s, half = j // 2, j % 2
                rows = slice(HD * half, HD * half + HD)
                c = s * P + HD * half
                hold(pe, bank_read[5], n.now(bank_read[5]))
                if half == 0:
                    hold(pe, bank_read[6], n.before(bank_read[6]))
                pe.matmul(ps[rows, 6, 0:SEQ], vA[:, 0, c:c + HD], p2T[:, 0:SEQ], start=True, stop=False,
                          skip_group_check=True)
                pe.matmul(ps[rows, 6, P:SEQ], vA[:, 1, c:c + HD], p2T[:, SEQ:SEQ + P], start=False, stop=True,
                          skip_group_check=True).then_inc(bank_full[6], 1)

            def level(h, l, bank, at):
                for blk in range(2):
                    mm = pe.matmul(ps[:, bank, at + HD * blk:at + HD * blk + HD], kl[:, l, blk * P:blk * P + P],
                                   ql[:, l, blk * HD:blk * HD + HD], start=True, stop=True)
                return mm

            def hgrn_scores(h, g):
                if g == 0:
                    hold(pe, bank_read[7], n.before(bank_read[7]))
                    pe.wait_ge(khs_ready, n.next(khs_ready))
                    pe.wait_ge(level_ready, n.next(level_ready, 2))
                    for blk in range(2):
                        pe.matmul(ps[:, 7, blk * P:blk * P + P], kh_s[:, h, blk * P:blk * P + P],
                                  qh[:, h, blk * P:blk * P + P], start=True, stop=True)
                    level(h, 0, 7, 256)
                    level(h, 1, 7, 384).then_inc(bank_full[7], 1)
                elif g == 1:
                    hold(pe, bank_read[3], n.before(bank_read[3]))
                    pe.wait_ge(level_ready, n.next(level_ready, 4))
                    for l in range(2, 6):
                        mm = level(h, l, 3, (l - 2) * P)
                    mm.then_inc(bank_full[3], 1)
                else:
                    hold(pe, bank_read[7], n.before(bank_read[7]))
                    pe.wait_ge(level_ready, n.next(level_ready, 2))
                    level(h, 6, 7, 0)
                    pe.matmul(ps[:, 7, P:2 * P], kx, qx, start=True, stop=True).then_inc(bank_full[7], 1)

            def hgrn_values(h):
                hold(pe, bank_read[7], n.now(bank_read[7]))
                hold(pe, bank_read[3], n.before(bank_read[3]))
                c = h * P
                pe.matmul(ps[:, 3, 0:SEQ], iN[:, 0, c:c + P], amat[:, 0:3:2, :], start=True, stop=False,
                          skip_group_check=True)
                pe.matmul(ps[:, 3, P:SEQ], iN[:, 1, c:c + P], amat[:, 1, :], start=False, stop=True,
                          skip_group_check=True).then_inc(bank_full[3], 1)

            for b in (2, 3):
                hold(pe, tile_read[b], STREAM.before("branch_a", 0, b))
            ya_first = n.now(bank_read[6])
            with pe.Fori(0, 4) as i:
                n.enter("heads2", i)

                def proj(t):
                    if t in (2, 3, 8, 9):
                        by_token("heads2", i, t, P * (t % 2), x2tok)
                    else:
                        tile("heads2", i, t, x2, SEQ)

                for t in range(6):
                    proj(t)
                hgrn_scores(0, 0)
                proj(6)
                rotate(i, q_r, 4)
                proj(7)
                hgrn_scores(0, 1)
                rotate(i, k_r, 6)
                proj(8)
                hgrn_scores(0, 2)
                proj(9)
                scores2(0)
                hgrn_values(0)
                proj(10)
                turn2(0)
                scores2(1)
                hgrn_scores(1, 0)
                proj(11)
                values2(0)
                turn2(1)
                scores2(2)
                proj(12)
                hgrn_scores(1, 1)
                values2(1)
                turn2(2)
                scores2(3)
                proj(13)
                hgrn_scores(1, 2)
                values2(2)
                turn2(3)
                proj(14)
                hgrn_values(1)
                values2(3)
                proj(15)
                n.leave(4)

            for b in (2, 3):
                hold(pe, bank_read[b], n.now(bank_read[b]))
            for t in range(4):
                tile("branch_a", 0, t, lambda k: ya[:, k, :], SEQ, ready=(bank_read[6], ya_first + 1))
            head_sums(lambda j: sq[:, j, 0:SEQ], SEQ, squared)
            for t in range(4, 8):
                tile("branch_a", 0, t, lambda k: ya[:, k, :], SEQ)
                if t == 5:
                    head_sums(lambda j: sq[:, 4 + j, 0:SEQ], SEQ, squared)
            for t in range(8):
                tile("branch_b", 0, t, lambda k: oh[:, k, :], SEQ, ready=(hgrn_ready, 1))
            for t in range(8):
                tile("mix_out2", 0, t, x2, SEQ, ready=(mixed, KB + 1))
            norm_sum(SEQ)

            def scores_x(h):
                hold(pe, bank_read[4], n.before(bank_read[4]))
                t = 2 * h + 1
                b = STREAM.bank("cross_q", t)
                pe.wait_ge(tile_read[b], STREAM.before("cross_q", 0, t) + 1)
                for blk in range(2):
                    for e in range(2):
                        mm = pe.matmul(ps[:, 4, blk * SEQ:(blk + 1) * SEQ], qX[:, 2 * h + e, blk * P:blk * P + P],
                                       k_mem[:, 2 * h + e, :], start=e == 0, stop=e == 1)
                mm.then_inc(bank_full[4], 1)

            def turn_x(h):
                pe.wait_ge(probs_ready, n.next(probs_ready))
                hold(pe, bank_read[5], n.before(bank_read[5]))
                for m in range(2):
                    for blk in range(2):
                        mm = pe.transpose(ps[:, 5, m * SEQ + blk * P:m * SEQ + blk * P + P],
                                          pX[:, blk, m * P:m * P + P], ident)
                mm.then_inc(bank_full[5], 1)

            def values_x(h):
                hold(pe, bank_read[5], n.now(bank_read[5]))
                hold(pe, bank_read[6], n.before(bank_read[6]))
                for e in range(2):
                    for m in range(2):
                        c = h * SEQ + e * P
                        mm = pe.matmul(ps[:, 6, e * SEQ:(e + 1) * SEQ], v_mem[:, m, c:c + P], pXT[:, m, :],
                                       start=m == 0, stop=m == 1)
                mm.then_inc(bank_full[6], 1)

            for h in range(4):
                tile("cross_q", 0, 2 * h, x2, SEQ, ready=(normed, NORMS["cross"] * KB + 1))
                tile("cross_q", 0, 2 * h + 1, x2, SEQ)
                if h >= 1:
                    scores_x(h - 1)
                if h >= 2:
                    turn_x(h - 2)
                    values_x(h - 2)
            turn_x(2)
            scores_x(3)
            values_x(2)
            turn_x(3)
            values_x(3)
            hold(pe, bank_read[6], n.now(bank_read[6]))
            for t in range(8):
                tile("cross_out", 0, t, lambda k: oX[:, k, :], SEQ)
            norm_sum(SEQ)
            ffn("up2", "down2", SEQ, 2)

        @block.scalar
        def _(sc):
            n = Tally("scalar")

            def act_fn(out, src, fn, sem_, **kw):
                ins = sc.activation(out, src, fn, **kw)
                ins.then_inc(sem_, 1)
                n.before(sem_)
                return ins

            def copy_tile(phase, i, t, out, src, scale=1.0, fn=ACT.Copy):
                b = STREAM.bank(phase, t)
                sc.wait_ge(tile_done, STREAM.done(phase, i, t))
                sc.activation(out, src, fn, scale=scale).then_inc(tile_read[b], 1)

            def root_of_mean(bank, width, count, eps, out, sem_):
                sc.wait_ge(bank_full[bank], n.next(bank_full[bank]))
                sc.activation(out, ps[:, bank, 0:width], ACT.Sqrt, bias=col(eps), scale=1.0 / count).then_inc(sem_, 1)

            def high_parts(phase, i, c, free):
                slot, p = STREAM.at[phase][5][c % len(STREAM.at[phase][5])], STREAM.parity(phase, c)
                sc.wait_ge(landed[slot], STREAM.landed(phase, i, c))
                if free is not None:
                    sc.wait_ge(tile_done, free)
                for half in (1, 0):
                    cols = slice(half * HALF_CHUNK, (half + 1) * HALF_CHUNK)
                    sc.activation(parts[:, p, cols], ring[:, slot, cols], ACT.Copy).then_inc(split_high, 1)

            def x_high_parts(dst, src, width, first):
                for k in range(KB):
                    sc.wait_ge(normed, first + k + 1)
                    sc.activation(dst[:, k, 0:width], src[:, k, 0:width], ACT.Copy).then_inc(x_high_ready, 1)

            sc.dma_start(table[:, :], a["table"]).then_inc(table_in, 16)
            sc.dma_start(mem[:, :, :], a["mem"]).then_inc(mem_in, 16)
            sc.wait_ge(res_in, 64)
            sc.wait_ge(table_in, 16)
            for k in range(KB):
                act_fn(sq[:, k, :], res[:, k, :], ACT.Square, squared)
            root_of_mean(4, T1, D, "eps6", root[:, :], rooted)
            sc.wait_ge(mem_in, 16)
            for k in range(KB):
                act_fn(k_mem[:, k, :], mem[:, k, :], ACT.Square, squared)
            x_high_parts(x_high, sq, T1, NORMS["mix1"] * KB)
            high_parts("heads1", 0, 0, None)
            high_parts("heads1", 0, 1, None)
            root_of_mean(4, SEQ, D, "eps6", root[:, 0:SEQ], rooted)
            x_high_parts(mem_high, k_mem, SEQ, NORMS["mem"] * KB)
            sc.wait_ge(consts_ready, 1)
            sc.activation(lam_t[:, 2:4], lam_t[:, 0:2], ACT.Exp).then_inc(lb_exp, 1)

            def exps1(u):
                width = META + P * (u % 2 + 1)
                sc.wait_ge(max_ready, n.next(max_ready))
                hold(sc, probs_ready, n.before(probs_ready))
                for m in range(2):
                    ins = sc.activation(E1[:, m, 0:width], ps[:, 4 + m, 0:width], ACT.Exp, bias=nmax[:, m:m + 1],
                                        accum_out=rsum[:, m:m + 1])
                ins.then_inc(bank_read[4], 1)

            def turned1(u):
                sc.wait_ge(bank_full[6], n.next(bank_full[6]))
                hold(sc, bank_full[7], n.now(bank_full[7]))
                sc.activation(a1M[0:META, :], ps[0:META, 6, 2 * P:3 * P], ACT.Copy)
                sc.activation(a1T[:, 0:P * (u % 2 + 1)], ps[:, 6, 0:P * (u % 2 + 1)], ACT.Copy).then_inc(bank_read[6], 1)

            def output1(i, u):
                h = u // 2
                sc.wait_ge(bank_full[7], n.next(bank_full[7]))
                sc.activation(att[:, i * 2 + h, LEAD + P * (u % 2):LEAD + P * (u % 2) + P], ps[:, 7, 0:P],
                              ACT.Copy).then_inc(bank_read[7], 1)

            with sc.Fori(0, 4) as i:
                n.enter("heads1", i)

                def ahead1(c):
                    high_parts("heads1", i, c + 2, STREAM.done("heads1", i, 2 * c + 1))

                def tanh1(t, out):
                    bk = STREAM.bank("heads1", t)
                    sc.wait_ge(tile_done, STREAM.done("heads1", i, t))
                    sc.activation(out, ps[:, bk, 0:out.shape[-1]], ACT.Tanh, scale=0.5).then_inc(tile_read[bk], 1)

                hold(sc, bank_full[4], n.before(bank_full[4], 4))
                for t in (0, 1):
                    copy_tile("heads1", i, t, qT[:, t, :], ps[:, STREAM.bank("heads1", t), 0:TQ], HD ** -0.5)
                ahead1(0)
                for t in (2, 3):
                    copy_tile("heads1", i, t, kT[:, t - 2, :], ps[:, STREAM.bank("heads1", t), 0:T1])
                ahead1(1)
                hold(sc, bank_full[7], n.now(bank_full[7]))
                copy_tile("heads1", i, 4, vN[:, 0, :], ps[:, STREAM.bank("heads1", 4), 0:CW])
                for t in range(4):
                    sc.wait_ge(tile_read[STREAM.bank("heads1", t)], STREAM.before("heads1", i, t) + 1)
                sc.activation(qM[:, bass.ds(i * 2, 2), :], qT[:, :, 0:LEAD], ACT.Copy)
                sc.activation(kM[:, bass.ds(i * 2, 2), :], kT[:, :, 0:META], ACT.Copy)
                sc.wait_ge(tile_done, STREAM.done("heads1", i, 5))
                bk = STREAM.bank("heads1", 5)
                sc.activation(vM[0:META, bass.ds(i * CW, CW)], ps[0:META, bk, CW:2 * CW], ACT.Copy)
                sc.activation(v_meta[0:META, :], ps[0:META, bk, CW:2 * CW], ACT.Copy).then_inc(kv_ready, 1)
                sc.activation(vN[:, 1, :], ps[:, bk, 0:CW], ACT.Copy).then_inc(tile_read[bk], 1)
                ahead1(2)
                exps1(0)
                hold(sc, tile_read[STREAM.bank("heads1", 9)], STREAM.before("heads1", i, 9))
                tanh1(6, tanh_b[:, 0, :])
                tanh1(7, tanh_b[:, 1, :])
                ahead1(3)
                turned1(0)
                exps1(1)
                ahead1(4)
                output1(i, 0)
                turned1(1)
                exps1(2)
                tanh1(10, gates[:, i * 2, :])
                tanh1(11, gates[:, i * 2 + 1, :])
                ahead1(5)
                output1(i, 1)
                turned1(2)
                exps1(3)
                tanh1(12, gates[:, i * 2 + KB, :])
                tanh1(13, gates[:, i * 2 + KB + 1, :])
                ahead1(6)
                output1(i, 2)
                turned1(3)
                copy_tile("heads1", i, 14, k_mem[:, i * 2, :], ps[:, STREAM.bank("heads1", 14), 0:SEQ])
                output1(i, 3)
                copy_tile("heads1", i, 15, k_mem[:, i * 2 + 1, :], ps[:, STREAM.bank("heads1", 15), 0:SEQ])
                ahead1(7)
                n.leave(4)
            sc.dma_start(pos_i, a["positions"]).then_inc(pos_in, 16)
            sc.wait_ge(meta_shift, 2)
            sc.activation(sM[0:LEAD, :, :], sM[0:LEAD, :, :], ACT.Exp).then_inc(meta_exp, 1)

            def mem_v(t):
                copy_tile("mem_v", 0, t, v_mem[:, t % 2, t // 2 * CW:(t // 2 + 1) * CW],
                          ps[:, STREAM.bank("mem_v", t), 0:CW])
                if t in (1, 3):
                    high_parts("mem_v", 0, t // 2 + 2, STREAM.done("mem_v", 0, t))

            mem_v(0)
            mem_v(1)
            mem_v(2)
            sc.wait_ge(bank_full[6], n.next(bank_full[6]))
            sc.activation(aMT[0:META, :, :], ps[0:META, 6, 0:LEAD * HEADS].rearrange("p (h q) -> p h q", q=LEAD),
                          ACT.Copy).then_inc(meta_T, 1)
            mem_v(3)
            sc.wait_ge(bank_full[7], n.next(bank_full[7]))
            sc.activation(att[:, :, 0:LEAD], ps[:, 7, 0:LEAD * HEADS].rearrange("p (h q) -> p h q", q=LEAD),
                          ACT.Copy).then_inc(bank_read[7], 1)
            sc.wait_ge(bank_read[7], 1 + 4 * 4 + 1)
            for h in range(HEADS):
                act_fn(sq[:, h, 0:TQ], att[:, h, :], ACT.Square, squared)
                if h == 3:
                    mem_v(4)
            n.next(bank_full[4])
            for j in range(4):
                root_of_mean(4 + j, TQ, P, "eps6", att_root[:, 0, j * TQ:(j + 1) * TQ], bank_read[4 + j])
            mem_v(5)
            for j in range(4):
                root_of_mean(4 + j, TQ, P, "eps6", att_root[:, 1, j * TQ:(j + 1) * TQ], bank_read[4 + j])
            mem_v(6)
            mem_v(7)
            for k in range(KB):
                sc.wait_ge(centered, k + 1)
                act_fn(sq[:, k, 0:TQ], conv[:, k, :], ACT.Square, squared)
            n.next(bank_full[4])
            root_of_mean(5, TQ, D, "eps5", root[:, 0:TQ], bank_read[5])
            for k in range(KB):
                sc.wait_ge(conv_scaled, k + 1)
                sc.activation(conv[:, k, :], conv[:, k, :], ACT.Silu, scale=col("conv_ln_w", k),
                              bias=col("conv_ln_b", k)).then_inc(conv_act, 1)

            def down_high(down, between=None):
                free = [STREAM.done(down, d // 4, d % 4) for d in range(8)] + [STREAM.done(down + "_end", 0, 0)]
                for d in range(9):
                    if d + 2 < 8:
                        high_parts(down, (d + 2) // 4, (d + 2) % 4, free[d])
                    else:
                        high_parts(down + "_end", 0, d + 2 - 8, free[d])
                    if between and d == 2:
                        between()

            def squares_of_sum(phase, src, up=None):
                for t in range(KB):
                    if up and t in (4, 6):
                        high_parts(up, 0, t // 2 - 2, STREAM.done(phase, 0, t - 1))
                    b = STREAM.bank(phase, t)
                    sc.wait_ge(tile_read[b], STREAM.before(phase, 0, t) + 1)
                    act_fn(sq[:, t, 0:src(t).shape[-1]], src(t), ACT.Square, squared)

            squares_of_sum("mix_out1", lambda t: res[:, t, Q0:T1], "up1")
            root_of_mean(4, TQ, D, "eps6", root[:, 0:TQ], rooted)
            x_high_parts(x_high, sq, TQ, NORMS["ffn1"] * KB)

            def ahead(phase, i, c, up):
                free = STREAM.done(phase, i, 2 * c + 1)
                if phase == up:
                    high_parts(up, i, c + 2, free)
                else:
                    high_parts("down" + up[-1], 0, c, free)

            def ffn_taps(up, weights):
                def group(phase, i, j, g):
                    hold(sc, act_ready[g % 2], n.before(act_ready[g % 2], 2))
                    for e in range(4):
                        t = 4 * (g % 2) * (phase == up) + e
                        w = j + e if e < 2 else j + (FT + e - 2)
                        bk = STREAM.bank(phase, t)
                        sc.wait_ge(tile_done, STREAM.done(phase, i, t))
                        act_fn(taps[:, 4 * (g % 2) + e, :], ps[:, bk, 0:SEQ], ACT.Identity, tap0,
                               scale=table[:, bass.ds(w * 3 + AT["ffn_dw_w"], 1)] if not isinstance(w, int) else col("ffn_dw_w", 3 * w),
                               bias=table[:, bass.ds(w + AT["ffn_dw_b"], 1)] if not isinstance(w, int) else col("ffn_dw_b", w))
                        if e == 1:
                            for x in range(2):
                                tx = 4 * (g % 2) * (phase == up) + x
                                sc.wait_ge(tile_read[STREAM.bank(phase, tx)], STREAM.before(phase, i, tx) + 1)
                                act_fn(silu_g[:, 2 * (g % 2) + x, :], taps[:, 4 * (g % 2) + x, :], ACT.Silu, gate_act)
                        if e % 2 == 1:
                            ahead(phase, i, t // 2, up)
                return group

            group = ffn_taps("up1", None)
            with sc.Fori(0, 5) as i:
                n.enter("up1", i)
                group("up1", i, i * 4, 0)
                group("up1", i, i * 4 + 2, 1)
                n.leave(5)
            group("up1_end", 0, 20, 0)

            def squares_after_down(down, src):
                for t in range(KB):
                    sc.wait_ge(tile_read[t // 2], STREAM.before(down + "_end", 0, t // 2) + 1)
                    act_fn(sq[:, t, 0:SEQ], src(t), ACT.Square, squared)

            def tables2():
                for k in range(2):
                    sc.wait_ge(angle_ready, k + 1)
                    sc.activation((sin, cos)[k], (sin, cos)[k], ACT.Sin).then_inc(rope_ready, 1)
                sc.wait_ge(consts_ready, 2)
                sc.activation(lb_t[:, 0:16], lb_t[:, 0:16], ACT.Exp).then_inc(lb_exp, 1)

            down_high("down1", tables2)
            squares_after_down("down1", lambda t: res[:, t, META:T1])
            root_of_mean(4, SEQ, D, "eps6", root[:, 0:SEQ], rooted)
            for k in range(KB):
                sc.wait_ge(normed, NORMS["final1"] * KB + k + 1)
                act_fn(sq[:, k, 0:SEQ], res2[:, k, :], ACT.Square, squared)
            root_of_mean(4, SEQ, D, "eps6", root[:, 0:SEQ], rooted)
            for t in range(KB):
                copy_tile("forget", 0, t, bT[:, t, :], ps[:, STREAM.bank("forget", t), 0:SEQ], fn=ACT.Sigmoid)
            sc.wait_ge(forget_ready, KB)
            sc.activation(conv_f[:, 0:KB * SEQ], conv_f[:, 0:KB * SEQ], ACT.Ln).then_inc(log_ready, 1)

            def reuse(x):
                hold(sc, level_ready, n.now(level_ready) - (x != 0))
                n.before(level_ready)

            def decay(x):
                sc.wait_ge(diff_ready, n.next(diff_ready))
                reuse(x)
                sc.activation(el[:, x % 2, :], dl[:, x % 2, :], ACT.Exp).then_inc(decay_ready, 1)

            def cross_decay(i, h):
                bh = bT[:, i * 2 + h, :]
                reuse(1)
                sc.activation(cross_e[:, 0, :], bh[:, 0:P], ACT.Exp, scale=-1.0, bias=bh[:, P - 1:P])
                sc.activation(cross_e[:, 1, :], bh[:, P:SEQ], ACT.Exp).then_inc(decay_ready, 1)

            def head_keys(i, h):
                sc.activation(kh_s[:, h, :], kh[:, i * 2 + h, :], ACT.Copy).then_inc(khs_ready, 1)

            def exps2(j):
                sc.wait_ge(max_ready, n.next(max_ready, 2))
                sc.activation(p2[:, 0:P], ps[:, 4, 0:P], ACT.Exp, bias=nmax[:, 0:1], accum_out=rsum[:, 0:1])
                sc.activation(p2[:, P:3 * P], ps[:, 4, P:3 * P], ACT.Exp, bias=nmax[:, 1:2],
                              accum_out=rsum[:, 1:2]).then_inc(bank_read[4], 1)

            def turned2():
                sc.wait_ge(bank_full[5], n.next(bank_full[5]))
                hold(sc, bank_full[6], n.now(bank_full[6]))
                sc.activation(p2T, ps[:, 5, 0:3 * P], ACT.Copy).then_inc(bank_read[5], 1)
                n.next(bank_full[6])

            def output2(i, s):
                sc.wait_ge(bank_full[6], n.now(bank_full[6]))
                sc.activation(ya[:, i * 2 + s, :], ps[:, 6, 0:SEQ], ACT.Copy).then_inc(bank_read[6], 1)

            def hgrn_output(i, h):
                n.next(bank_full[3])
                sc.wait_ge(bank_full[3], n.next(bank_full[3]))
                sc.activation(oh[:, i * 2 + h, :], ps[:, 3, 0:SEQ], ACT.Copy).then_inc(bank_read[3], 1)

            sc.wait_ge(cum_ready, HEADS)
            with sc.Fori(0, 4) as i:
                n.enter("heads2", i)

                def copy2(t, out, width=SEQ, **kw):
                    copy_tile("heads2", i, t, out, ps[:, STREAM.bank("heads2", t), 0:width], **kw)

                def tanh2(t, out, sem_):
                    sc.wait_ge(tile_done, STREAM.done("heads2", i, t))
                    sc.activation(out, ps[:, STREAM.bank("heads2", t), 0:SEQ], ACT.Tanh, scale=0.5).then_inc(sem_, 1)

                tanh2(0, tanh_q[:, 0, :], tanh_ready)
                tanh2(1, tanh_q[:, 1, :], tanh_ready)
                hold(sc, bank_full[7], n.before(bank_full[7], 4))
                decay(0)
                decay(1)
                hold(sc, bank_full[3], n.now(bank_full[3]))
                copy2(2, iN[:, 0, :])
                copy2(3, iN[:, 1, :])
                head_keys(i, 0)
                head_keys(i, 1)
                decay(2)
                decay(3)
                hold(sc, bank_full[4], n.before(bank_full[4], 4))
                copy2(4, q_r[:, 0, :], scale=HD ** -0.5)
                copy2(5, q_r[:, 1, :], scale=HD ** -0.5)
                decay(4)
                decay(5)
                copy2(6, k_r[:, 0, :])
                copy2(7, k_r[:, 1, :])
                decay(6)
                cross_decay(i, 0)
                hold(sc, bank_full[6], n.now(bank_full[6]))
                copy2(8, vA[:, 0, :])
                copy2(9, vA[:, 1, :])
                exps2(0)
                decay(7)
                decay(8)
                hgrn_output(i, 0)
                copy2(10, gates[:, i * 2, 0:SEQ], fn=ACT.Tanh, scale=0.5)
                turned2()
                exps2(1)
                for x in range(9, 13):
                    decay(x)
                copy2(11, gates[:, i * 2 + 1, 0:SEQ], fn=ACT.Tanh, scale=0.5)
                turned2()
                exps2(2)
                decay(13)
                cross_decay(i, 1)
                copy2(12, gates[:, i * 2 + KB, 0:SEQ], fn=ACT.Tanh, scale=0.5)
                output2(i, 0)
                turned2()
                exps2(3)
                copy2(13, gates[:, i * 2 + KB + 1, 0:SEQ], fn=ACT.Tanh, scale=0.5)
                turned2()
                tanh2(14, tanh_o[:, 0, :], tanh_ready)
                hgrn_output(i, 1)
                output2(i, 1)
                tanh2(15, tanh_o[:, 1, :], tanh_ready)
                n.leave(4)
            sc.wait_ge(bank_read[3], 1 + 2 * HEADS)
            for h in range(HEADS):
                act_fn(sq[:, h, 0:SEQ], oh[:, h, :], ACT.Square, squared)
            for g in range(2):
                for j in range(4):
                    root_of_mean(4 + j, SEQ, P, "eps6", head_root[:, g, j * SEQ:(j + 1) * SEQ], bank_read[4 + j])
            squares_of_sum("mix_out2", lambda t: res2[:, t, :])
            root_of_mean(4, SEQ, D, "eps6", root[:, 0:SEQ], rooted)

            def exps_x(h):
                sc.wait_ge(max_ready, n.next(max_ready))
                for blk in range(2):
                    ins = sc.activation(pX[:, blk, :], ps[:, 4, blk * SEQ:(blk + 1) * SEQ], ACT.Exp,
                                        bias=nmax[:, blk:blk + 1], accum_out=rsum[:, blk:blk + 1])
                ins.then_inc(bank_read[4], 1)

            def turned_x(h):
                sc.wait_ge(bank_full[5], n.next(bank_full[5]))
                hold(sc, bank_full[6], n.now(bank_full[6]))
                sc.activation(pXT.rearrange("p a b -> p (a b)"), ps[:, 5, :], ACT.Copy).then_inc(bank_read[5], 1)

            def output_x(h):
                sc.wait_ge(bank_full[6], n.next(bank_full[6]))
                sc.activation(oX[:, 2 * h:2 * h + 2, :], ps[:, 6, :].rearrange("p (e t) -> p e t", t=SEQ), ACT.Copy)\
                  .then_inc(bank_read[6], 1)

            def query_x(h):
                for t in (2 * h, 2 * h + 1):
                    copy_tile("cross_q", 0, t, qX[:, t, :], ps[:, STREAM.bank("cross_q", t), 0:SEQ], SEQ ** -0.5)

            query_x(0)
            query_x(1)
            exps_x(0)
            query_x(2)
            turned_x(0)
            exps_x(1)
            output_x(0)
            query_x(3)
            turned_x(1)
            exps_x(2)
            output_x(1)
            turned_x(2)
            exps_x(3)
            output_x(2)
            turned_x(3)
            output_x(3)
            n.next(bank_full[4], 4)
            squares_of_sum("cross_out", lambda t: res2[:, t, :], "up2")
            root_of_mean(4, SEQ, D, "eps6", root[:, 0:SEQ], rooted)
            x_high_parts(x_high, sq, SEQ, NORMS["ffn2"] * KB)

            def gates2(phase, i, g):
                for x in range(2):
                    t = 4 * (g % 2) * (phase == "up2") + x
                    bv = STREAM.bank(phase, t + 2)
                    hold(sc, tile_read[bv], STREAM.before(phase, i, t + 2))
                    b = STREAM.bank(phase, t)
                    sc.wait_ge(tile_done, STREAM.done(phase, i, t))
                    sc.activation(silu_g[:, 2 * (g % 2) + x, :], ps[:, b, 0:SEQ], ACT.Silu).then_inc(tile_read[b], 1)
                for c in range(2):
                    ahead(phase, i, 2 * g + c, "up2")

            with sc.Fori(0, 5) as i:
                gates2("up2", i, 0)
                gates2("up2", i, 1)
            gates2("up2_end", 0, 0)
            down_high("down2")
            squares_after_down("down2", lambda t: res2[:, t, :])
            root_of_mean(4, SEQ, D, "eps6", root[:, 0:SEQ], rooted)

        @block.vector
        def _(ve):
            n = Tally("vector")

            def step(ins):
                ins.then_inc(dve_step, 1)
                ve.wait_ge(dve_step, n.next(dve_step))

            def norm(width, src, dst, weight, roots):
                ve.wait_ge(rooted, roots)
                step(ve.reciprocal(rinv[:, 0:width], root[:, 0:width]))
                for k in range(KB):
                    ve.scalar_tensor_tensor(dst(k), src(k), col(weight, k), rinv[:, 0:width], ALU.mult, ALU.mult)\
                      .then_inc(normed, 1)

            def x_low_parts(dst, src, high, width, name):
                for k in range(KB):
                    ve.wait_ge(x_high_ready, INPUTS[name] * KB + k + 1)
                    ve.tensor_tensor(dst[:, k, 0:width], src[:, k, 0:width], high[:, k, 0:width].bitcast(F32), ALU.subtract)\
                      .then_inc(x_low_ready, 1)

            ve.wait_ge(table_in, 16)
            ve.memset(glu[:, :, 0:TAPS - 1], 0.0)
            norm(T1, lambda k: res[:, k, :], lambda k: sq[:, k, :], "norm_mix_w", 1)
            x_low_parts(x_low1, sq, x_high, T1, "mix1")
            lam = col("lambdas", 0, 4 * HD)
            step(ve.tensor_tensor(lam[:, 0:HD], lam[:, 0:HD], lam[:, HD:2 * HD], ALU.mult))
            step(ve.tensor_tensor(lam[:, 2 * HD:3 * HD], lam[:, 2 * HD:3 * HD], lam[:, 3 * HD:4 * HD], ALU.mult))
            step(ve.reduce_sum(lam_t[:, 0:1], lam[:, 0:HD], AX))
            ve.reduce_sum(lam_t[:, 1:2], lam[:, 2 * HD:3 * HD], AX).then_inc(consts_ready, 1)
            cw = col("conv_dw_w", 0, KB * TAPS)
            step(ve.tensor_scalar(cw, cw, 0.5, None, ALU.mult))
            step(ve.tensor_scalar(sub_w, col("subln_w"), 1.0 - LAMBDA_INIT, None, ALU.mult))
            norm(SEQ, lambda k: mem[:, k, :], lambda k: k_mem[:, k, :], "norm_mem_g_2", 2)
            x_low_parts(mem_low, k_mem, mem_high, SEQ, "mem")
            ve.wait_ge(lb_exp, 1)
            step(ve.tensor_tensor(neg_lam, lam_t[:, 3:4], lam_t[:, 2:3], ALU.subtract))
            step(ve.tensor_scalar(neg_lam, neg_lam, -LAMBDA_INIT, None, ALU.add))

            def maxima1(u):
                width = META + P * (u % 2 + 1)
                ve.wait_ge(bank_full[4], n.next(bank_full[4]))
                step(ve.memset(ps[0:CHUNK, 4:6, width - CHUNK:width], NEG))
                ve.tensor_reduce(nmax, ps[:, 4:6, 0:width], AX, ALU.max, negate=True).then_inc(max_ready, 1)

            def combine1(u):
                width = META + P * (u % 2 + 1)
                ve.wait_ge(bank_read[4], n.next(bank_read[4]))
                step(ve.reciprocal(rden, rsum))
                step(ve.tensor_tensor(coef[:, 0:1], rden[:, 1:2], neg_lam, ALU.mult))
                hold(ve, bank_full[6], n.before(bank_full[6]))
                step(ve.tensor_scalar(a1[:, 0:width], E1[:, 0, 0:width], rden[:, 0:1], None, ALU.mult))
                ve.scalar_tensor_tensor(a1[:, 0:width], E1[:, 1, 0:width], coef[:, 0:1], a1[:, 0:width],
                                        ALU.mult, ALU.add).then_inc(probs_ready, 1)

            def glu1(i, h):
                b, g = STREAM.bank("heads1", 8 + h), STREAM.bank("heads1", 6 + h)
                ve.wait_ge(tile_read[g], STREAM.before("heads1", i, 6 + h) + 1)
                ve.wait_ge(tile_done, STREAM.done("heads1", i, 8 + h))
                ve.scalar_tensor_tensor(glu[:, i * 2 + h, TAPS - 1:TAPS - 1 + T1], tanh_b[:, h, :], 1.0,
                                        ps[:, b, 0:T1], ALU.add, ALU.mult).then_inc(tile_read[b], 1)

            def conv1(j, first=0, end=TAPS):
                def w(k):
                    return table[:, bass.ds(j * TAPS + (AT["conv_dw_w"] + k), 1)]

                def u(k):
                    return glu[:, j, Q0 + k:Q0 + k + TQ]

                sums = [conv[:, j, :], conv_odd]
                if first == 0:
                    hold(ve, conv_ready, n.now(conv_ready))
                    ve.tensor_scalar(sums[0], u(0), w(0), table[:, bass.ds(j + AT["conv_dw_b"], 1)], ALU.mult, ALU.add)\
                      .then_inc(dve_step, 1)
                    n.next(dve_step)
                    ve.tensor_scalar(sums[1], u(1), w(1), None, ALU.mult).then_inc(dve_step, 1)
                else:
                    n.before(dve_step, -1)
                for k in range(max(first, 2), end):
                    ve.wait_ge(dve_step, n.now(dve_step))
                    ve.scalar_tensor_tensor(sums[k % 2], u(k), w(k), sums[k % 2], ALU.mult, ALU.add).then_inc(dve_step, 1)
                    n.next(dve_step)
                ve.wait_ge(dve_step, n.next(dve_step))
                if end == TAPS:
                    ve.tensor_tensor(sums[0], sums[0], sums[1], ALU.add).then_inc(conv_ready, 1)
                    n.before(conv_ready)

            def pair1(i):
                maxima1(0)
                combine1(0)
                maxima1(1)
                combine1(1)
                glu1(i, 0)
                glu1(i, 1)
                ve.wait_ge(tile_read[STREAM.bank("heads1", 9)], STREAM.before("heads1", i, 9) + 1)
                conv1(i * 2, 0, 8)
                maxima1(2)
                combine1(2)
                conv1(i * 2, 8, 16)
                maxima1(3)
                combine1(3)
                conv1(i * 2, 16, TAPS)

            n.next(bank_full[4], 2)
            with ve.Fori(0, 3) as i:
                n.enter("heads1", i)
                pair1(i)
                conv1(i * 2 + 1)
                n.leave(3)
            pair1(3)

            ve.wait_ge(bank_full[4], n.next(bank_full[4]))
            for m in range(2):
                s_m = ps[0:LEAD, 4 + m, 0:HEADS * META].rearrange("p (h k) -> p h k", k=META)
                top = m_max[:, m * HEADS:(m + 1) * HEADS]
                step(ve.tensor_reduce(top, s_m, AX, ALU.max))
                ve.tensor_tensor(sM[0:LEAD, m * HEADS:(m + 1) * HEADS, :], s_m, spread(top, META), ALU.subtract)\
                  .then_inc(meta_shift, 1)
            conv1(7, 0, 10)
            ve.wait_ge(meta_exp, 1)
            step(ve.reduce_sum(m_sum, sM[0:LEAD, :, :], AX))
            step(ve.reciprocal(m_sum, m_sum))
            step(ve.tensor_tensor(sM[0:LEAD, :, :], sM[0:LEAD, :, :], spread(m_sum, META), ALU.mult))
            ve.scalar_tensor_tensor(aM[0:LEAD, :, :], sM[0:LEAD, HEADS:, :], neg_lam[0:LEAD, :], sM[0:LEAD, 0:HEADS, :],
                                    ALU.mult, ALU.add).then_inc(meta_probs, 1)
            conv1(7, 10, TAPS)
            ve.wait_ge(bank_full[4], n.next(bank_full[4], 3))
            for k in range(KB):
                ve.scalar_tensor_tensor(conv[:, k, :], ps[:, 4, 0:TQ], -1.0 / D, conv[:, k, :], ALU.mult, ALU.add)\
                  .then_inc(centered, 1)
            ve.wait_ge(bank_read[7], 1 + 4 * 4 + 1 + 2)
            for g in range(2):
                heads = att[:, 4 * g:4 * g + 4, :].rearrange("p h t -> p (h t)")
                r_g = att_root[:, g, :]
                step(ve.reciprocal(r_g, r_g))
                step(ve.scalar_tensor_tensor(heads, heads, sub_w, r_g, ALU.mult, ALU.mult))
                ve.scalar_tensor_tensor(heads, gates[:, 4 * g:4 * g + 4, :].rearrange("p h t -> p (h t)"), 1.0, heads,
                                        ALU.add, ALU.mult).then_inc(att_gated, 1)
            ve.wait_ge(bank_read[5], 1 + 2 + 1)
            step(ve.reciprocal(rinv[:, 0:TQ], root[:, 0:TQ]))
            for k in range(KB):
                ve.tensor_tensor(conv[:, k, :], conv[:, k, :], rinv[:, 0:TQ], ALU.mult).then_inc(conv_scaled, 1)
            ve.wait_ge(att_gated, 2)
            for t in range(KB):
                b = STREAM.bank("conv_out", t)
                ve.wait_ge(tile_done, STREAM.done("conv_out", 0, t))
                ve.scalar_tensor_tensor(xT[:, t, 0:TQ], gates[:, KB + t, :], 1.0, ps[:, b, 0:TQ], ALU.add, ALU.mult)\
                  .then_inc(tile_read[b], 1)
                ve.wait_ge(tile_read[b], STREAM.before("conv_out", 0, t) + 1)
                ve.tensor_tensor(xT[:, t, 0:TQ], xT[:, t, 0:TQ], att[:, t, :], ALU.add).then_inc(mixed, 1)

            def add_tiles(phase, dst, width, up=None):
                for t in range(KB):
                    if up and t in (5, 7):
                        low_half(ve, up, 0, (t - 5) // 2, 0)
                    b = STREAM.bank(phase, t)
                    ve.wait_ge(tile_done, STREAM.done(phase, 0, t))
                    ve.scalar_tensor_tensor(dst(t), ps[:, b, 0:width], HALF[phase], dst(t), ALU.mult, ALU.add)\
                      .then_inc(tile_read[b], 1)

            HALF = {"mix_out1": 0.5, "mix_out2": 0.5, "cross_out": 1.0}
            def low_v(phase, i, c):
                low_half(ve, phase, i, c, 0)

            def down_low(down, between=None):
                for d in range(2, 8):
                    low_v(down, d // 4, d % 4)
                    if between and d == 3:
                        between()
                for d in range(3):
                    low_v(down + "_end", 0, d)

            add_tiles("mix_out1", lambda t: res[:, t, Q0:T1], TQ, "up1")
            norm(TQ, lambda k: res[:, k, Q0:T1], lambda k: sq[:, k, 0:TQ], "norm_ffn_w", 3)
            x_low_parts(x_low, sq, x_high, TQ, "ffn1")

            def behind(phase, i, c, up):
                if phase == up:
                    low_v(up, i, c + 2)
                else:
                    low_v("down" + up[-1], 0, c)

            def group1(phase, i, j, g):
                for e in range(4):
                    t = 4 * (g % 2) * (phase == "up1") + e
                    w = j + e if e < 2 else j + (FT + e - 2)
                    b = STREAM.bank(phase, t)
                    acc = taps[:, 4 * (g % 2) + e, :]

                    def tap(k):
                        return table[:, bass.ds(w * 3 + (AT["ffn_dw_w"] + k), 1)] if not isinstance(w, int) else \
                            col("ffn_dw_w", 3 * w + k)

                    ve.wait_ge(tap0, n.next(tap0))
                    step(ve.scalar_tensor_tensor(acc, ps[:, b, 1:SEQ + 1], tap(1), acc, ALU.mult, ALU.add))
                    ve.scalar_tensor_tensor(acc, ps[:, b, 2:SEQ + 2], tap(2), acc, ALU.mult, ALU.add)\
                      .then_inc(tile_read[b], 1)
                    if e >= 2:
                        ve.wait_ge(tile_read[b], STREAM.before(phase, i, t) + 1)
                        ve.wait_ge(gate_act, n.next(gate_act))
                        ve.tensor_tensor(branch[:, j + (e - 2), 0:SEQ], silu_g[:, 2 * (g % 2) + e - 2, :], acc, ALU.mult)\
                          .then_inc(act_ready[g % 2], 1)
                    if e % 2 == 1:
                        behind(phase, i, t // 2, "up1")

            with ve.Fori(0, 5) as i:
                n.enter("up1", i)
                group1("up1", i, i * 4, 0)
                group1("up1", i, i * 4 + 2, 1)
                n.leave(5)
            group1("up1_end", 0, 20, 0)

            def add_down(down, dst):
                for b in range(4):
                    ve.wait_ge(tile_done, STREAM.done(down + "_end", 0, 2 + b))
                    ve.tensor_tensor(dst(b), ps[:, b, :].rearrange("p (t s) -> p t s", s=SEQ), dst(b), ALU.add)\
                      .then_inc(tile_read[b], 1)


            def tables1():
                ve.wait_ge(pos_in, 16)
                ang, turns, over = rope_a, rope_b, rope_c
                step(ve.tensor_copy(turns, pos_i))
                step(ve.tensor_scalar(ang, turns, col("inv_freq"), None, ALU.mult))
                step(ve.tensor_scalar(turns, ang, 0.15915494309189535, MAGIC, ALU.mult, ALU.add))
                step(ve.tensor_scalar(turns, turns, -MAGIC, None, ALU.add))
                for part in TWO_PI:
                    step(ve.scalar_tensor_tensor(ang, turns, -part, ang, ALU.mult, ALU.add))
                ve.tensor_scalar(sin, ang, -PI_IN, PI_IN, ALU.max, ALU.min).then_inc(angle_ready, 1)
                step(ve.tensor_scalar(ang, ang, 1.5707963267948966, None, ALU.add))
                step(ve.tensor_scalar(over, ang, 3.141592653589793, -6.283185307179586, ALU.is_gt, ALU.mult))
                step(ve.tensor_tensor(ang, ang, over, ALU.add))
                ve.tensor_scalar(cos, ang, -PI_IN, PI_IN, ALU.max, ALU.min).then_inc(angle_ready, 1)
                l0, l1 = col("lb_logits", 0, KB), col("lb_logits", KB, KB)
                step(ve.tensor_tensor(lb_t[:, 16:24], l0, l1, ALU.max))
                ve.tensor_tensor(lb_t[:, 0:8], l0, lb_t[:, 16:24], ALU.subtract)
                ve.tensor_tensor(lb_t[:, 8:16], l1, lb_t[:, 16:24], ALU.subtract).then_inc(consts_ready, 1)
                ve.wait_ge(lb_exp, 2)
                step(ve.tensor_tensor(lb_t[:, 16:24], lb_t[:, 0:8], lb_t[:, 8:16], ALU.add))
                step(ve.reciprocal(lb_t[:, 16:24], lb_t[:, 16:24]))
                step(ve.tensor_tensor(lb, lb_t[:, 0:8], lb_t[:, 16:24], ALU.mult))
                step(ve.tensor_scalar(one_lb, lb, -1.0, 1.0, ALU.mult, ALU.add))
                step(ve.tensor_scalar(hgrn_g, col("hgrn_norm_g_2", 0, KB), 0.5, None, ALU.mult))

            down_low("down1", tables1)
            add_down("down1", lambda b: res[:, 2 * b:2 * b + 2, META:T1])
            norm(SEQ, lambda k: res[:, k, META:T1], lambda k: res2[:, k, :], "norm_final_w", 4)

            norm(SEQ, lambda k: res2[:, k, :], lambda k: xT[:, k, 0:SEQ], "norm_mix_g_2", 5)
            for t in range(KB):
                b = STREAM.bank("forget", t)
                ve.wait_ge(tile_read[b], STREAM.before("forget", 0, t) + 1)
                step(ve.tensor_scalar(bT[:, t, :], bT[:, t, :], one_lb[:, t:t + 1], lb[:, t:t + 1], ALU.mult, ALU.add))
                step(ve.tensor_scalar(kh[:, t, :], bT[:, t, :], -KEY_SCALE, KEY_SCALE, ALU.mult, ALU.add))
                ve.tensor_scalar(bT[:, t, :], bT[:, t, :], LOG_MIN, None, ALU.max).then_inc(forget_ready, 1)
            ve.wait_ge(log_ready, 1)
            with ve.Fori(0, HEADS) as i:
                n.enter("cumulate", i)
                for half in range(2):
                    part = bT[:, i, half * P:half * P + P]
                    ins = ve.tensor_tensor_scan(part, ones, part, 0.0, ALU.mult, ALU.add)
                ins.then_inc(cum_ready, 1)
                n.leave(HEADS)

            masks = col("level_masks", 0, len(LEVELS) * P).bitcast(I32).rearrange("p (l c) -> p l c", c=P)

            def halves(x, m):
                return x.rearrange("p (b u m) -> p b u m", u=2, m=m)

            def level(i, h, x):
                l, m = x % 7, LEVELS[x % 7]
                ve.wait_ge(decay_ready, n.next(decay_ready))
                e = halves(el[:, x % 2, :], m)
                ve.tensor_tensor(halves(kl[:, l, :], m)[:, :, 0, :], halves(kh[:, i * 2 + h, :], m)[:, :, 0, :],
                                 e[:, :, 0, :], ALU.mult)
                ve.tensor_tensor(ql[:, l, :].rearrange("p (b m) -> p b m", m=m), halves(qh[:, h, :], m)[:, :, 1, :],
                                 e[:, :, 1, :], ALU.mult).then_inc(level_ready, 1)

            def cross_level(i, h):
                ve.wait_ge(decay_ready, n.next(decay_ready))
                ve.tensor_tensor(kx, kh[:, i * 2 + h, 0:P], cross_e[:, 0, :], ALU.mult)
                ve.tensor_tensor(qx, qh[:, h, P:SEQ], cross_e[:, 1, :], ALU.mult).then_inc(level_ready, 1)

            diag = amat[:, 0:2, :].rearrange("p a b -> p (a b)")

            def place(l, bank, at, sem_):
                m = LEVELS[l]
                ve.sem_inc(place_waited, 1)
                ins = ve.copy_predicated(halves(diag, m)[:, :, 1, :], masks[:, l, :].rearrange("p (b m) -> p b m", m=m),
                                         ps[:, bank, at:at + P].rearrange("p (b m) -> p b m", m=m))
                ins.then_inc(sem_, 1)
                ve.wait_ge(sem_, n.next(sem_))

            def gather0():
                hold(ve, bank_full[3], n.now(bank_full[3]))
                ve.wait_ge(bank_full[7], n.next(bank_full[7]))
                step(ve.tensor_tensor(amat[:, 0:2, :], ps[:, 7, 0:SEQ].rearrange("p (a b) -> p a b", b=P),
                                      ident.rearrange("p (o b) -> p o b", o=1).to_broadcast([P, 2, P]), ALU.mult))
                place(0, 7, 256, dve_step)
                place(1, 7, 384, bank_read[7])

            def gather1():
                ve.wait_ge(bank_full[3], n.next(bank_full[3]))
                for l in range(2, 6):
                    place(l, 3, (l - 2) * P, bank_read[3] if l == 5 else dve_step)

            def gather2():
                ve.wait_ge(bank_full[7], n.next(bank_full[7]))
                place(6, 7, 0, dve_step)
                ve.tensor_copy(amat[:, 2, :], ps[:, 7, P:2 * P]).then_inc(bank_read[7], 1)
                n.before(bank_read[7])
                n.before(bank_full[3])

            def rope2(x, bank):
                ve.wait_ge(bank_full[bank], n.next(bank_full[bank]))
                wide = lambda y: y.rearrange("p (o t) -> p o t", o=1).to_broadcast([P, 2, SEQ])
                step(ve.tensor_tensor(rope_t, ps[:, bank, :].rearrange("p (a t) -> p a t", t=SEQ), wide(sin), ALU.mult))
                step(ve.tensor_tensor(x, x, wide(cos), ALU.mult))
                ve.tensor_tensor(x, x, rope_t, ALU.add).then_inc(bank_read[bank], 1)

            def maxima2(j):
                ve.wait_ge(bank_full[4], n.next(bank_full[4]))
                blocks = ps[:, 4, 0:4 * P].rearrange("p (a b) -> p a b", b=P)[:, 0:3:2, :]
                step(ve.tensor_tensor(blocks, blocks, col("causal", 0, P).rearrange("p (o b) -> p o b", o=1).to_broadcast([P, 2, P]),
                                      ALU.add))
                ve.tensor_reduce(nmax[:, 0:1], ps[:, 4, 0:P], AX, ALU.max, negate=True).then_inc(max_ready, 1)
                ve.tensor_reduce(nmax[:, 1:2], ps[:, 4, P:3 * P], AX, ALU.max, negate=True).then_inc(max_ready, 1)

            def normalise2():
                ve.wait_ge(bank_read[4], n.next(bank_read[4]))
                step(ve.reciprocal(rden, rsum))
                ve.tensor_scalar(p2[:, 0:P], p2[:, 0:P], rden[:, 0:1], None, ALU.mult)
                ve.tensor_scalar(p2[:, P:3 * P], p2[:, P:3 * P], rden[:, 1:2], None, ALU.mult).then_inc(probs_ready, 1)

            def silu2(i, t, x, tanh, out):
                b = STREAM.bank("heads2", t)
                ve.wait_ge(tanh_ready, n.next(tanh_ready))
                ve.scalar_tensor_tensor(out, tanh, 1.0, ps[:, b, 0:SEQ], ALU.add, ALU.mult).then_inc(tile_read[b], 1)

            n.next(bank_full[4], 3)
            n.next(bank_full[7], 4 * 4 + 3)
            n.next(bank_read[4], 2)
            n.next(bank_read[7], 4 * 4 + 3)
            ve.wait_ge(rope_ready, 2)
            with ve.Fori(0, 4) as i:
                n.enter("heads2", i)
                hold(ve, bank_full[7], n.now(bank_full[7]))
                silu2(i, 0, 0, tanh_q[:, 0, :], qh[:, 0, :])
                silu2(i, 1, 0, tanh_q[:, 1, :], qh[:, 1, :])
                ve.wait_ge(tile_read[1], STREAM.before("heads2", i, 1) + 1)
                for x in range(4):
                    level(i, 0, x)
                rope2(q_r, 2)
                gather0()
                level(i, 0, 4)
                level(i, 0, 5)
                rope2(k_r, 2)
                level(i, 0, 6)
                cross_level(i, 0)
                gather1()
                maxima2(0)
                gather2()
                normalise2()
                level(i, 1, 7)
                level(i, 1, 8)
                maxima2(1)
                normalise2()
                gather0()
                for x in range(9, 13):
                    level(i, 1, x)
                maxima2(2)
                normalise2()
                maxima2(3)
                gather1()
                level(i, 1, 13)
                cross_level(i, 1)
                normalise2()
                gather2()
                silu2(i, 14, 0, tanh_o[:, 0, :], og[:, i * 2, :])
                silu2(i, 15, 0, tanh_o[:, 1, :], og[:, i * 2 + 1, :])
                n.leave(4)
            def gate_a(ts):
                for t in ts:
                    b = STREAM.bank("branch_a", t)
                    ve.wait_ge(tile_done, STREAM.done("branch_a", 0, t))
                    ve.scalar_tensor_tensor(xT[:, t, 0:SEQ], gates[:, t, 0:SEQ], 1.0, ps[:, b, 0:SEQ], ALU.add, ALU.mult)\
                      .then_inc(tile_read[b], 1)

            gate_a(range(4))
            for g in range(2):
                if g == 1:
                    gate_a(range(4, 8))
                ve.wait_ge(bank_read[7], n.next(bank_read[7]))
                step(ve.reciprocal(head_root[:, g, :], head_root[:, g, :]))
                for j in range(4):
                    h = 4 * g + j
                    step(ve.scalar_tensor_tensor(oh[:, h, :], oh[:, h, :], hgrn_g[:, h:h + 1],
                                                 head_root[:, g, j * SEQ:(j + 1) * SEQ], ALU.mult, ALU.mult))
                    ve.tensor_tensor(oh[:, h, :], oh[:, h, :], og[:, h, :], ALU.mult).then_inc(hgrn_ready, 1)
            for t in range(KB):
                b = STREAM.bank("branch_b", t)
                ve.wait_ge(tile_done, STREAM.done("branch_b", 0, t))
                ve.scalar_tensor_tensor(branch_t[:, t % 2, :], gates[:, KB + t, 0:SEQ], 1.0, ps[:, b, 0:SEQ], ALU.add, ALU.mult)\
                  .then_inc(tile_read[b], 1)
                ve.wait_ge(tile_read[b], STREAM.before("branch_b", 0, t) + 1)
                ve.tensor_tensor(xT[:, t, 0:SEQ], xT[:, t, 0:SEQ], branch_t[:, t % 2, :], ALU.add).then_inc(mixed, 1)
            add_tiles("mix_out2", lambda t: res2[:, t, :], SEQ)
            norm(SEQ, lambda k: res2[:, k, :], lambda k: xT[:, k, 0:SEQ], "norm_x_g_2", 6)
            n.next(bank_full[4], 3)
            n.next(bank_read[4], 2)

            for h in range(4):
                ve.wait_ge(bank_full[4], n.next(bank_full[4]))
                ve.tensor_reduce(nmax, ps[:, 4, :].rearrange("p (b m) -> p b m", m=SEQ), AX, ALU.max, negate=True)\
                  .then_inc(max_ready, 1)
                ve.wait_ge(bank_read[4], n.next(bank_read[4]))
                step(ve.reciprocal(rden, rsum))
                ve.tensor_scalar(pX[:, 0, :], pX[:, 0, :], rden[:, 0:1], None, ALU.mult)
                ve.tensor_scalar(pX[:, 1, :], pX[:, 1, :], rden[:, 1:2], None, ALU.mult).then_inc(probs_ready, 1)
            add_tiles("cross_out", lambda t: res2[:, t, :], SEQ, "up2")
            norm(SEQ, lambda k: res2[:, k, :], lambda k: sq[:, k, 0:SEQ], "norm_ffn_g_2", 7)
            x_low_parts(x_low, sq, x_high, SEQ, "ffn2")

            def group2(phase, i, j, g):
                for x in range(2):
                    t = 4 * (g % 2) * (phase == "up2") + x
                    b, bg = STREAM.bank(phase, t + 2), STREAM.bank(phase, t)
                    ve.wait_ge(tile_read[bg], STREAM.before(phase, i, t) + 1)
                    ve.wait_ge(tile_done, STREAM.done(phase, i, t + 2))
                    ve.tensor_tensor(branch[:, j + x, 0:SEQ], silu_g[:, 2 * (g % 2) + x, :], ps[:, b, 0:SEQ], ALU.mult)\
                      .then_inc(tile_read[b], 1)
                for c in range(2):
                    behind(phase, i, 2 * (g % 2) * (phase == "up2") + c, "up2")

            with ve.Fori(0, 5) as i:
                n.enter("up2", i)
                group2("up2", i, i * 4, 0)
                group2("up2", i, i * 4 + 2, 1)
                n.leave(5)
            group2("up2_end", 0, 20, 0)
            down_low("down2")
            add_down("down2", lambda b: res2[:, 2 * b:2 * b + 2, :])
            norm(SEQ, lambda k: res2[:, k, :], lambda k: xT[:, k, 0:SEQ], "final_norm_g_2", 8)


        @block.gpsimd
        def _(gp):
            n = Tally("gpsimd")

            def low_g(phase, i, c):
                low_half(gp, phase, i, c, 1)

            def hidden_parts(j):
                for x in range(2):
                    gp.tensor_copy(act_high[:, j + x, :], branch[:, j + x, 0:SEQ]).then_inc(hidden_high, 1)
                for x in range(2):
                    gp.wait_ge(hidden_high, n.next(hidden_high))
                    gp.sem_inc(diff_waited, 1)
                    gp.tensor_tensor(act_low[:, j + x, 0:SEQ], branch[:, j + x, 0:SEQ], act_high[:, j + x, :].bitcast(F32), ALU.subtract)\
                      .then_inc(hidden_low, 1)

            def ffn_parts(up, down, made):
                low_g(up, 0, 0)
                low_g(up, 0, 1)
                with gp.Fori(0, 5) as i:
                    n.enter(up, i)
                    for g in range(2):
                        low_g(up, i, 2 * g + 2)
                        low_g(up, i, 2 * g + 3)
                        made(up, i, g)
                        hidden_parts(i * 4 + 2 * g)
                    n.leave(5)
                low_g(down, 0, 0)
                low_g(down, 0, 1)
                made(up + "_end", 0, 0)
                hidden_parts(20)
                for d in range(2, 8):
                    low_g(down, d // 4, d % 4)
                for d in range(3):
                    low_g(down + "_end", 0, d)

            def made1(phase, i, g):
                gp.wait_ge(act_ready[g], n.next(act_ready[g], 2))

            def made2(phase, i, g):
                for t in (4 * g + 2, 4 * g + 3):
                    gp.wait_ge(tile_read[STREAM.bank(phase, t)], STREAM.before(phase, i, t) + 1)

            def both(phase, i, c):
                low_half(gp, phase, i, c, 1)
                low_half(gp, phase, i, c, 0)

            with gp.Fori(0, 4) as i:
                for c in range(8):
                    both("heads1", i, c)
            for c in range(4):
                both("mem_v", 0, c)
            ffn_parts("up1", "down1", made1)
            gp.wait_ge(cum_ready, HEADS)
            gp.memset(kl, 0.0).then_inc(pool_step, 1)
            gp.wait_ge(pool_step, n.next(pool_step))
            with gp.Fori(0, 4) as i:
                n.enter("heads2", i)
                for x in range(14):
                    m = LEVELS[x % 7]
                    b = bT[:, i * 2 + x // 7, :].rearrange("p (b u m) -> p b u m", u=2, m=m)
                    d = dl[:, x % 2, :].rearrange("p (b u m) -> p b u m", u=2, m=m)
                    middle = b[:, :, 0, m - 1:m].to_broadcast([P, P // m, m])
                    hold(gp, decay_ready, n.now(decay_ready) - (x != 0))
                    n.before(decay_ready, 1 + (x % 7 == 6))
                    gp.sem_inc(diff_waited, 1)
                    gp.tensor_tensor(d[:, :, 0, :], middle, b[:, :, 0, :], ALU.subtract)
                    gp.tensor_tensor(d[:, :, 1, :], b[:, :, 1, :], middle, ALU.subtract).then_inc(diff_ready, 1)
                n.leave(4)
            ffn_parts("up2", "down2", made2)


def tabled(w, tiles):
    return w.reshape(tiles, P).T


def chunks_of(w, columns):
    k, m = w.shape
    v = w.reshape(k // P, P, m)
    return [v[:, :, c:c + CW].transpose(1, 0, 2).reshape(P, -1) for c in columns]


def kernel(**inputs):
    import numpy as np
    import concourse.bacc as bacc
    from concourse.bass_utils import run_bass_kernel_spmd

    x = {name: np.asarray(value) for name, value in inputs.items()}

    every = list(range(0, D, CW))
    w1, w2 = x["w_in"][0], x["w_in_2"][0]
    stream = []
    for i in range(4):
        stream += chunks_of(w1, [s * D + i * CW for s in (0, 1, 2, 4, 3, 5, 6)])
        stream += chunks_of(x["wkv_x_2"][0], [i * CW])
    stream += chunks_of(x["wkv_x_2"][0], [D + c for c in every])
    stream += chunks_of(x["w_conv_out"][0], every) + chunks_of(x["w_out"][0], every)

    def ffn(up, down):
        for j in range(0, FF, CW):
            stream.extend(chunks_of(up, [j, FF + j]))
        v = down.reshape(FT // 2, 2, P, D)
        stream.extend(v[c].transpose(1, 0, 2).reshape(P, -1) for c in range(FT // 2))

    ffn(x["w_up"][0], x["w_down"][0])
    stream += chunks_of(w2, [4 * D + c for c in every])
    for i in range(4):
        stream += chunks_of(w2, [s * D + i * CW for s in (3, 5, 0, 1, 2, 7, 8, 6)])
    for name in ("w_br_attn_2", "w_br_hgrn_2", "w_out_2", "wq_x_2", "wo_x_2"):
        stream += chunks_of(x[name][0], every)
    ffn(x["w_ffn_in_2"][0], x["w_ffn_out_2"][0])
    weights = np.stack(stream)

    t = np.zeros((P, TABLE_W), np.float32)

    def put(name, value):
        t[:, AT[name]:AT[name] + WIDTH[name]] = value

    for name in ("norm_mix_w", "conv_dw_b", "conv_ln_w", "conv_ln_b", "norm_ffn_w", "norm_final_w", "norm_mix_g_2",
                 "hgrn_norm_g_2", "norm_x_g_2", "norm_mem_g_2", "norm_ffn_g_2", "final_norm_g_2"):
        put(name, tabled(x[name].reshape(-1), KB))
    put("subln_w", x["subln_w"].reshape(P, 1))
    put("conv_dw_w", x["conv_dw_w"][0].reshape(TAPS, KB, P).transpose(2, 1, 0).reshape(P, -1))
    put("ffn_dw_w", x["ffn_dw_w"][0].reshape(3, 2 * FT, P).transpose(2, 1, 0).reshape(P, -1))
    put("ffn_dw_b", tabled(x["ffn_dw_b"].reshape(-1), 2 * FT))
    put("lb_logits", x["hgrn_lb_logits_2"].reshape(2, KB, P).transpose(2, 0, 1).reshape(P, -1))
    lambdas = np.concatenate([x[name].reshape(-1) for name in ("lambda_q1", "lambda_k1", "lambda_q2", "lambda_k2")])
    put("lambdas", np.broadcast_to(lambdas, (P, 4 * HD)))

    p, q = np.arange(P)[:, None], np.arange(P)[None, :]
    put("ones", 1.0)
    put("ident", p == q)
    put("rotate", np.where(p == q + HD // 2, -1.0, 0.0) * (q % HD < HD // 2) + np.where(p == q - HD // 2, 1.0, 0.0) * (q % HD >= HD // 2))
    put("inv_freq", 10000.0 ** (-2.0 * (p % (HD // 2)) / HD))
    put("eps6", 1e-6)
    put("eps5", 1e-5)
    put("causal", np.where(q <= p, 0.0, NEG))
    masks = []
    for m in LEVELS:
        column = np.arange(P // 2)[None, :] // m
        one = ((p // (2 * m) == column) & (p % (2 * m) < m)).astype(np.float32)
        masks += [one, one]
    put("level_masks", np.concatenate(masks, 1))

    h = np.concatenate([x["meta_tokens"], x["x"][0]], 0)
    arrays = {
        "weights": weights,
        "table": t,
        "h_in": np.ascontiguousarray(h.T.reshape(KB, P, T1).transpose(1, 0, 2)),
        "mem": np.ascontiguousarray(x["mem_2"][0].T.reshape(KB, P, SEQ).transpose(1, 0, 2)),
        "positions": np.ascontiguousarray(np.broadcast_to(x["positions_2"].astype(np.int32), (P, SEQ))),
    }
    nc = bacc.Bacc("TRN2", target_bir_lowering=False, num_devices=1)
    aps = {}
    for name, value in arrays.items():
        dt = mybir.dt.from_np(value.dtype)
        aps[name] = nc.dram_tensor(name, value.shape, dt, kind="ExternalInput").ap()
    aps["out"] = nc.dram_tensor("out", (P, KB, SEQ), F32, kind="ExternalOutput").ap()
    blocks_kernel(nc, aps)
    r = run_bass_kernel_spmd(nc, [arrays], core_ids=[0])
    y = np.asarray(r.results[0]["out"])
    return y.transpose(1, 0, 2).reshape(D, SEQ).T[None]
```
